# Optimizing a Trainium2 kernel written in Bass

```python
import math
import jax, jax.numpy as jnp
from jax import lax
import numpy as np

D_MODEL = 1024
BATCH = 1
SEQ = 512
DEPTH = 2

GRID_W = 64
CTX_LEN = 256
HEAD_DIM = 64
NA_HEADS = 4
NA_ROWS = 8
NA_COLS = 16
MLA_HEADS = 4
MLA_Q_LORA = 256
MLA_KV_LORA = 192
MLA_NOPE = 64
MLA_ROPE = 32
MLA_V = 64
SG_GROUPS = 4
SG_CHUNK = 128
SG_WIDTH = 256
GQA_HEADS = 4
GQA_KV_HEADS = 2
N_BRANCH = 4
BRANCH_WIDTH = 256
FFN_DIM = 2816
CONV_WIDTH = 3

Q_BLOCK = 128
ROPE_THETA = 10000.0
EPS = 1e-6
NEG_INF = -1e30

NA_IN = 3 * NA_HEADS * HEAD_DIM
MLA_IN = MLA_Q_LORA + MLA_KV_LORA + MLA_ROPE
SG_IN = 2 * SG_WIDTH
GQA_IN = (GQA_HEADS + 2 * GQA_KV_HEADS) * HEAD_DIM
IN_WIDTH = NA_IN + MLA_IN + SG_IN + GQA_IN

kernel_name = "hybrid_natten_mla_gmlp_gqa_diffusion_block"

def rms(x):
    xf = x.astype(jnp.float32)
    return (xf * lax.rsqrt(jnp.mean(xf * xf, axis=-1, keepdims=True) + EPS)).astype(x.dtype)

def rope_1d(x, pos):
    half = x.shape[-1] // 2
    inv = ROPE_THETA ** (-jnp.arange(half, dtype=jnp.float32) / half)
    ang = pos.astype(jnp.float32)[:, None] * inv[None, :]
    shape = (ang.shape[0],) + (1,) * (x.ndim - 3) + (half,)
    cos = jnp.cos(ang).reshape(shape).astype(x.dtype)
    sin = jnp.sin(ang).reshape(shape).astype(x.dtype)
    x1, x2 = x[..., :half], x[..., half:]
    return jnp.concatenate([x1 * cos - x2 * sin, x2 * cos + x1 * sin], axis=-1)

def rope_2d(x, rows, cols):
    h = x.shape[-1] // 2
    return jnp.concatenate([rope_1d(x[..., :h], rows), rope_1d(x[..., h:], cols)], axis=-1)

def modulate(x, shift, scale):
    return rms(x) * (1 + scale[:, None]) + shift[:, None]

def softmax_f32(s):
    return jax.nn.softmax(s.astype(jnp.float32), axis=-1)

def prep_na(z, p):
    B, T, _ = z.shape
    qkv = z.reshape(B, T, 3, NA_HEADS, HEAD_DIM)
    q = rms(qkv[:, :, 0]) * p['na_q_norm']
    k = rms(qkv[:, :, 1]) * p['na_k_norm']
    return q, k, qkv[:, :, 2]

def prep_mla(z, p, pos):
    B, T, _ = z.shape
    cq, ckv, k_rope = jnp.split(z, [MLA_Q_LORA, MLA_Q_LORA + MLA_KV_LORA], axis=-1)
    q = ((rms(cq) * p['mla_cq_norm']) @ p['mla_w_uq']).reshape(B, T, MLA_HEADS, MLA_NOPE + MLA_ROPE)
    kv = ((rms(ckv) * p['mla_ckv_norm']) @ p['mla_w_ukv']).reshape(B, T, MLA_HEADS, MLA_NOPE + MLA_V)
    qg, kg = p['mla_q_norm'], p['mla_k_norm']
    q_nope = rms(q[..., :MLA_NOPE]) * qg[:MLA_NOPE]
    q_rope = rms(q[..., MLA_NOPE:]) * qg[MLA_NOPE:]
    k_nope = rms(kv[..., :MLA_NOPE]) * kg[:MLA_NOPE]
    k_rope = rms(k_rope) * kg[MLA_NOPE:]
    v = kv[..., MLA_NOPE:]
    if pos is not None:
        q_rope = rope_2d(q_rope, *pos)
        k_rope = rope_2d(k_rope, *pos)
    q = jnp.concatenate([q_nope, q_rope], axis=-1)[:, :, :, None]
    k = jnp.concatenate([k_nope, jnp.broadcast_to(k_rope[:, :, None], (B, T, MLA_HEADS, MLA_ROPE))], axis=-1)
    return q, k, v

def prep_gqa(z, p, pos):
    B, T, _ = z.shape
    q, k, v = jnp.split(z, [GQA_HEADS * HEAD_DIM, (GQA_HEADS + GQA_KV_HEADS) * HEAD_DIM], axis=-1)
    q = rms(q.reshape(B, T, GQA_KV_HEADS, GQA_HEADS // GQA_KV_HEADS, HEAD_DIM)) * p['gqa_q_norm']
    k = rms(k.reshape(B, T, GQA_KV_HEADS, HEAD_DIM)) * p['gqa_k_norm']
    v = v.reshape(B, T, GQA_KV_HEADS, HEAD_DIM)
    if pos is not None:
        q = rope_2d(q, *pos)
        k = rope_2d(k, *pos)
    return q, k, v

def token_mixing_inputs(h, p, pos):
    z = h @ p['w_in']
    z_na, z_mla, z_sg, z_gqa = jnp.split(z, [NA_IN, NA_IN + MLA_IN, NA_IN + MLA_IN + SG_IN], axis=-1)
    return prep_na(z_na, p), prep_mla(z_mla, p, pos), z_sg, prep_gqa(z_gqa, p, pos)

def attend_ctx(q, k, v, scale):
    s = jnp.einsum('bqgrd,bkgd->bgrqk', q, k) * scale
    p = softmax_f32(s).astype(v.dtype)
    o = jnp.einsum('bgrqk,bkgv->bqgrv', p, v)
    return o.reshape(o.shape[0], o.shape[1], -1)

def attend_latent_blocked(q, k_lat, v_lat, k_ctx, v_ctx, scale):
    B, T, G, R, dq = q.shape
    k_all = jnp.concatenate([k_ctx, k_lat], axis=1)
    v_all = jnp.concatenate([v_ctx, v_lat], axis=1)
    nblk = T // Q_BLOCK
    qb = jnp.moveaxis(q.reshape(B, nblk, Q_BLOCK, G, R, dq), 1, 0)

    def one_block(q_blk):
        s = jnp.einsum('bqgrd,bkgd->bgrqk', q_blk, k_all) * scale
        p = softmax_f32(s).astype(v_all.dtype)
        return jnp.einsum('bgrqk,bkgv->bqgrv', p, v_all)

    o = lax.map(one_block, qb)
    return jnp.moveaxis(o, 0, 1).reshape(B, T, -1)

def neighbourhood_attention(q, k, v, k_ctx, v_ctx, rpb, rows):
    B, T, H, d = q.shape
    kr, kc = min(NA_ROWS, rows), NA_COLS
    scale = d ** -0.5
    qg = q.reshape(B, rows, GRID_W, H, d)
    kg = k.reshape(B, rows, GRID_W, H, d)
    vg = v.reshape(B, rows, GRID_W, H, d)
    r = jnp.arange(rows)
    row_idx = jnp.clip(r - kr // 2, 0, rows - kr)[:, None] + jnp.arange(kr)[None, :]
    col = jnp.arange(GRID_W)
    c_start = jnp.clip(col - kc // 2, 0, GRID_W - kc)
    col_mask = (col[None, :] >= c_start[:, None]) & (col[None, :] < c_start[:, None] + kc)
    k_band = kg[:, row_idx]
    v_band = vg[:, row_idx]
    s_nb = (jnp.einsum('brqhd,brkwhd->bhrqkw', qg, k_band) * scale).astype(jnp.float32)
    dr = row_idx - r[:, None] + (NA_ROWS - 1)
    dc = jnp.clip(col[None, :] - col[:, None] + (NA_COLS - 1), 0, 2 * NA_COLS - 2)
    bias = jnp.take(rpb[:, dr], dc, axis=-1).transpose(0, 1, 3, 2, 4)
    s_nb = jnp.where(col_mask[:, None, :], s_nb + bias.astype(jnp.float32), NEG_INF)
    s_nb = s_nb.reshape(B, H, rows, GRID_W, kr * GRID_W)
    s_cx = (jnp.einsum('brqhd,bkhd->bhrqk', qg, k_ctx) * scale).astype(jnp.float32)
    p = softmax_f32(jnp.concatenate([s_nb, s_cx], axis=-1))
    p_nb = p[..., :kr * GRID_W].reshape(B, H, rows, GRID_W, kr, GRID_W).astype(v.dtype)
    p_cx = p[..., kr * GRID_W:].astype(v.dtype)
    o = (jnp.einsum('bhrqkw,brkwhd->brqhd', p_nb, v_band)
         + jnp.einsum('bhrqk,bkhd->brqhd', p_cx, v_ctx))
    return o.reshape(B, T, H * d)

def spatial_gating(z_sg, p):
    B, T, _ = z_sg.shape
    uv = jax.nn.gelu(z_sg)
    u, v = uv[..., :SG_WIDTH], uv[..., SG_WIDTH:]
    v = rms(v) * p['sg_v_norm']
    vc = v.reshape(B, T // SG_CHUNK, SG_CHUNK, SG_GROUPS, SG_WIDTH // SG_GROUPS)
    mixed = jnp.einsum('gpq,bnqgc->bnpgc', p['sg_w_s'], vc) + p['sg_b_s'].T[None, None, :, :, None]
    return u * mixed.reshape(B, T, SG_WIDTH)

def merge_branches(h, branches, p):
    y = 0
    for i, o in enumerate(branches):
        y = y + jax.nn.sigmoid(h @ p['w_gate'][i] + p['b_gate'][i]) * (o @ p['w_branch'][i])
    return y @ p['w_out']

def dwconv3(x, w, b):
    xp = jnp.pad(x, ((0, 0), (1, 1), (0, 0)))
    return xp[:, :-2] * w[0] + xp[:, 1:-1] * w[1] + xp[:, 2:] * w[2] + b

def conv_ffn(h, p):
    up = dwconv3(h @ p['w_up'], p['conv_w'], p['conv_b'])
    a, g = jnp.split(up, 2, axis=-1)
    return (jax.nn.silu(g) * a) @ p['w_down']

def layer(x, cx, c, c_ctx, p, pos, ctx_out):
    rows = x.shape[1] // GRID_W
    mod = jax.nn.silu(c) @ p['w_ada'] + p['b_ada']
    mod_c = (jax.nn.silu(c_ctx) @ p['w_ada'] + p['b_ada'])[None]
    sh1, sc1, g1, sh2, sc2, g2 = jnp.split(mod, 6, axis=-1)
    csh1, csc1, cg1, csh2, csc2, cg2 = jnp.split(mod_c, 6, axis=-1)

    h = modulate(x, sh1, sc1)
    hc = modulate(cx, csh1, csc1)
    na, mla, sg, gqa = token_mixing_inputs(h, p, pos)
    na_c, mla_c, sg_c, gqa_c = token_mixing_inputs(hc, p, None)

    o_na = neighbourhood_attention(na[0], na[1], na[2], na_c[1], na_c[2], p['na_rpb'], rows)
    o_mla = attend_latent_blocked(mla[0], mla[1], mla[2], mla_c[1], mla_c[2], (MLA_NOPE + MLA_ROPE) ** -0.5)
    o_sg = spatial_gating(sg, p)
    o_gqa = attend_latent_blocked(gqa[0], gqa[1], gqa[2], gqa_c[1], gqa_c[2], HEAD_DIM ** -0.5)
    x = x + g1[:, None] * merge_branches(h, (o_na, o_mla, o_sg, o_gqa), p)
    x = x + g2[:, None] * conv_ffn(modulate(x, sh2, sc2), p)

    if ctx_out:
        oc_na = attend_ctx(na_c[0][:, :, :, None], na_c[1], na_c[2], HEAD_DIM ** -0.5)
        oc_mla = attend_ctx(mla_c[0], mla_c[1], mla_c[2], (MLA_NOPE + MLA_ROPE) ** -0.5)
        oc_sg = spatial_gating(sg_c, p)
        oc_gqa = attend_ctx(gqa_c[0], gqa_c[1], gqa_c[2], HEAD_DIM ** -0.5)
        cx = cx + cg1[:, None] * merge_branches(hc, (oc_na, oc_mla, oc_sg, oc_gqa), p)
        cx = cx + cg2[:, None] * conv_ffn(modulate(cx, csh2, csc2), p)
    return x, cx

def setup_inputs(seed: int = 0) -> dict:
    key = jax.random.key(seed)
    ks = jax.random.split(key, 32)
    L, D = DEPTH, D_MODEL

    def nrm(k, shape, fan_in):
        return jax.random.normal(k, shape, jnp.float32) * fan_in ** -0.5

    def gain(k, shape):
        return 1.0 + 0.02 * jax.random.normal(k, shape, jnp.float32)

    def small(k, shape):
        return 0.02 * jax.random.normal(k, shape, jnp.float32)

    return {
        'x': jax.random.normal(ks[0], (BATCH, SEQ, D), jnp.float32),
        'c': jax.random.normal(ks[1], (BATCH, D), jnp.float32),
        'ctx': jax.random.normal(ks[2], (BATCH, CTX_LEN, D), jnp.float32),
        'c_ctx': jax.random.normal(ks[3], (D,), jnp.float32),
        'w_ada': nrm(ks[4], (L, D, 6 * D), D),
        'b_ada': small(ks[5], (L, 6 * D)),
        'w_in': nrm(ks[6], (L, D, IN_WIDTH), D),
        'na_q_norm': gain(ks[7], (L, HEAD_DIM)),
        'na_k_norm': gain(ks[8], (L, HEAD_DIM)),
        'na_rpb': small(ks[9], (L, NA_HEADS, 2 * NA_ROWS - 1, 2 * NA_COLS - 1)),
        'mla_cq_norm': gain(ks[10], (L, MLA_Q_LORA)),
        'mla_ckv_norm': gain(ks[11], (L, MLA_KV_LORA)),
        'mla_w_uq': nrm(ks[12], (L, MLA_Q_LORA, MLA_HEADS * (MLA_NOPE + MLA_ROPE)), MLA_Q_LORA),
        'mla_w_ukv': nrm(ks[13], (L, MLA_KV_LORA, MLA_HEADS * (MLA_NOPE + MLA_V)), MLA_KV_LORA),
        'mla_q_norm': gain(ks[14], (L, MLA_NOPE + MLA_ROPE)),
        'mla_k_norm': gain(ks[15], (L, MLA_NOPE + MLA_ROPE)),
        'sg_v_norm': gain(ks[16], (L, SG_WIDTH)),
        'sg_w_s': nrm(ks[17], (L, SG_GROUPS, SG_CHUNK, SG_CHUNK), SG_CHUNK),
        'sg_b_s': gain(ks[18], (L, SG_GROUPS, SG_CHUNK)),
        'gqa_q_norm': gain(ks[19], (L, HEAD_DIM)),
        'gqa_k_norm': gain(ks[20], (L, HEAD_DIM)),
        'w_branch': nrm(ks[21], (L, N_BRANCH, BRANCH_WIDTH, D), BRANCH_WIDTH),
        'w_gate': nrm(ks[22], (L, N_BRANCH, D, D), D),
        'b_gate': small(ks[23], (L, N_BRANCH, D)),
        'w_out': nrm(ks[24], (L, D, D), D),
        'w_up': nrm(ks[25], (L, D, 2 * FFN_DIM), D),
        'conv_w': nrm(ks[26], (L, CONV_WIDTH, 2 * FFN_DIM), CONV_WIDTH),
        'conv_b': small(ks[27], (L, 2 * FFN_DIM)),
        'w_down': nrm(ks[28], (L, FFN_DIM, D), FFN_DIM),
    }

def reference(x, c, ctx, c_ctx, w_ada, b_ada, w_in, na_q_norm, na_k_norm, na_rpb,
              mla_cq_norm, mla_ckv_norm, mla_w_uq, mla_w_ukv, mla_q_norm, mla_k_norm,
              sg_v_norm, sg_w_s, sg_b_s, gqa_q_norm, gqa_k_norm,
              w_branch, w_gate, b_gate, w_out, w_up, conv_w, conv_b, w_down):
    T = x.shape[1]
    t = jnp.arange(T)
    pos = (t // GRID_W, t % GRID_W)
    cx = ctx
    for l in range(DEPTH):
        p = {
            'w_ada': w_ada[l], 'b_ada': b_ada[l], 'w_in': w_in[l],
            'na_q_norm': na_q_norm[l], 'na_k_norm': na_k_norm[l], 'na_rpb': na_rpb[l],
            'mla_cq_norm': mla_cq_norm[l], 'mla_ckv_norm': mla_ckv_norm[l],
            'mla_w_uq': mla_w_uq[l], 'mla_w_ukv': mla_w_ukv[l],
            'mla_q_norm': mla_q_norm[l], 'mla_k_norm': mla_k_norm[l],
            'sg_v_norm': sg_v_norm[l], 'sg_w_s': sg_w_s[l], 'sg_b_s': sg_b_s[l],
            'gqa_q_norm': gqa_q_norm[l], 'gqa_k_norm': gqa_k_norm[l],
            'w_branch': w_branch[l], 'w_gate': w_gate[l], 'b_gate': b_gate[l], 'w_out': w_out[l],
            'w_up': w_up[l], 'conv_w': conv_w[l], 'conv_b': conv_b[l], 'w_down': w_down[l],
        }
        x, cx = layer(x, cx, c, c_ctx, p, pos, l < DEPTH - 1)
    return x


_drawn_inputs = setup_inputs


def setup_inputs(seed=0):
    import zlib

    import numpy as np

    out = dict(_drawn_inputs(seed))
    spreads = {}
    factors = {'na_q_norm': 8.0,
     'na_k_norm': 8.0,
     'na_rpb': 64.0,
     'mla_cq_norm': 8.0,
     'mla_ckv_norm': 8.0,
     'mla_q_norm': 8.0,
     'mla_k_norm': 8.0,
     'sg_v_norm': 7.727,
     'sg_b_s': 7.7,
     'gqa_q_norm': 8.0,
     'gqa_k_norm': 8.0,
     'b_gate': 8.0,
     'conv_b': 3.675}
    for name, (base, spread) in spreads.items():
        noise = np.random.default_rng([zlib.crc32(name.encode()), seed]).standard_normal(out[name].shape)
        drawn = base * np.exp(spread * noise) if base else spread * noise
        out[name] = __import__('jax').numpy.asarray(drawn.astype(out[name].dtype))
    for name, factor in factors.items():
        out[name] = (out[name] * factor).astype(out[name].dtype)
    return out
```

```python
from contextlib import ExitStack

import concourse.bass as bass
from concourse import mybir

F32 = mybir.dt.float32
F32R = mybir.dt.float32r
ALU = mybir.AluOpType
ACT = mybir.ActivationFunctionType
AX = mybir.AxisListType

P = 128
D = 1024
KT = D // P
SEQ, CTX = 512, 256
T = SEQ + CTX
DEPTH = 2
GRID_W = 64
HD = 64
NHEAD = 4
FFN_T = 22
GROUPS = (8, 8, 6)
NBR = 4
BW = KT * P
MLA_K = 96
EPS = 1e-6
NAW = 896
NA_WIN = ((0, 256, 0), (0, 384, 256), (128, 384, 256), (256, 256, 640))

B_MLA, B_NA, B_GS = 6, 6, 9
B_IN = B_MLA + B_NA + B_GS
B_MERGE = KT * (NBR + 1)
B_LAYER = B_IN + B_MERGE + KT + 2 * FFN_T + KT * len(GROUPS)
N_BLOCKS = DEPTH * B_LAYER
ADA_T = 6 * KT
ADA_1 = 2 * KT
ADA_SLOTS = 7

C_NAQ, C_NAK, C_GQ, C_GK, C_MQ, C_MK, C_CQ, C_CKV, C_BG = 0, 1, 2, 3, 4, 5, 6, 8, 10
C_W0, C_W1, C_W2, C_CB = (C_BG + NBR * KT + 2 * FFN_T * i for i in range(4))
N_PAR = C_CB + 2 * FFN_T
M_ONE, M_256, M_192, M_64, M_MLA, M_ID = range(6)
SH1, SC1, G1, SH2, SC2, G2 = (KT * i for i in range(6))

PH_ADA, PH_NORM1, PH_MLA, PH_NA, PH_GS, PH_SG, PH_MERGE, PH_OUT, PH_NORM2, PH_FFN = 0, 1, 2, 4, 6, 8, 9, 10, 11, 12
PHASES = PH_FFN + 2 * len(GROUPS)

ROT_MLA = [(i // 16) * 16 + (i + 8) % 16 for i in range(32)]
ROT_GQA = [(i + 16) % 32 for i in range(32)]

SIGNALS = """
w_hi w_lo block_done sub_gemm phase_pe phase_act phase_dve
ada_used mod_step silu_c cc_loaded par_loaded const_loaded sg_loaded bias_loaded mask_loaded mask_step
adab_loaded cb_silu mod_acc mod_fold x_loaded x_reloaded x_spilled out_stored
sq ss y0 newton norm_u norm_v norm_hi norm_lo
in_zn in_hi in_lo h_perm rope_step kr_copy tok_done tok_copy
scores s_tab s_max s_nm s_exp s_rinv s_norm s_tr s_pt s_pv s_hi s_lo
sg_u sg_sq sg_y0 sg_step sg_vn sg_mix sg_add sg_o sg_hi sg_lo
br_copy gate_sig gate_mul gate_add y_hi y_lo out_add
up_lin up_tap up_conv up_act up_mul up_hi up_lo down_add""".split()


class Base:

    def __init__(self):
        self.v = {}

    def __getitem__(self, name):
        return self.v.get(name, 0)

    def advance(self, **counts):
        for name, n in counts.items():
            self.v[name] = self.v.get(name, 0) + n


def width(l):
    return T if l < DEPTH - 1 else SEQ


def mod_tiles(l):
    return (ADA_T, 2) if l < DEPTH - 1 else (ADA_T - ADA_1, 1)


def segs(w):
    return [(0, SEQ), (SEQ, CTX)] if w == T else [(0, SEQ)]


def tasks(kind, l):
    out = []
    for h in range(NHEAD):
        for j in range(SEQ // P):
            if kind == "na":
                k0, n, tc = NA_WIN[j]
                out.append((h, j * P, [(k0, n), (SEQ, CTX)], tc))
            else:
                out.append((h, j * P, [(0, SEQ), (SEQ, CTX)], None))
        if width(l) == T:
            for j in range(CTX // P):
                out.append((h, SEQ + j * P, [(SEQ, CTX)], None))
    return out


class Item:

    def __init__(self, to, src, rows, w, gain, idx=0, rope=None, z=None):
        self.to, self.src, self.rows, self.w, self.gain, self.idx, self.rope = to, src, rows, w, gain, idx, rope
        self.z = len(src) if z is None else z


def items(kind, l):
    w = width(l)
    if kind == "mla":
        return ([Item("cq", [(0, 0, P, M_256), (1, 0, P, M_256)], (0, P), w, C_CQ),
                 Item("ckv", [(2, 0, P, M_192), (3, 0, HD, M_192)], (0, P), T, C_CKV),
                 Item("kr", [(3, 64, 96, M_MLA)], (64, 96), T, C_MK, rope=2)]
                + [Item("mq", [(4 + h, 0, P, M_MLA)], (0, P), w, C_MQ, h, rope=2) for h in range(NHEAD)]
                + [Item("mk", [(8 + h, 0, HD, M_64)], (0, HD), T, C_MK, h) for h in range(NHEAD)])
    if kind == "na":
        return ([Item("nq", [(t, 0, P, M_64)], (0, P), w, C_NAQ, t, z=len(segs(w))) for t in range(2)]
                + [Item("nk", [(2 + t, 0, P, M_64)], (0, P), T, C_NAK, t, z=2) for t in range(2)])
    return ([Item("gq", [(t, 0, P, M_64)], (0, P), w, C_GQ, t, rope=0) for t in range(2)]
            + [Item("gk", [(2, 0, P, M_64)], (0, P), T, C_GK, 0, rope=0)])


def tile_widths(kind, l):
    w = width(l)
    return {"mla": [w, w, T, T] + [w] * 4 + [T] * 4, "na": [w, w, T, T], "gs": [w, w, T]}[kind]


def events(kind):
    g, s = (lambda t: ("gemm", t)), (lambda i: ("stat", i))
    if kind == "mla":
        return [g(0), g(1), g(2), s(0), g(3), s(1), s(2), g(4), g(5), s(3), g(6), s(4), g(7), s(5), g(8), s(6),
                g(9), s(7), g(10), s(8), g(11), s(9), s(10)]
    if kind == "na":
        return [g(0), g(1), s(0), g(2), s(1), g(3), s(2), s(3)]
    return [g(0), g(1), s(0), g(2), s(1), s(2)]


def block_of(kind, t):
    if kind == "mla" and t >= 4:
        return (4, t == 7) if t < 8 else (5, False)
    return t, True


def in_counts(kind, l):
    its = items(kind, l)
    return dict(sq=sum(len(i.src) for i in its), ss=len(its), y0=len(its), newton=3 * len(its),
                in_zn=sum(i.z for i in its), in_hi=4 * (kind == "mla"), in_lo=4 * (kind == "mla"),
                rope_step=4 * sum(i.rope is not None for i in its), kr_copy=3 * (kind == "mla"),
                sub_gemm=7 * (kind == "mla"), h_perm=2 * KT * (kind == "na"), tok_copy=2 if kind == "gs" else 1, sg_u=2 * (kind == "gs"))


def att_counts(kind, l):
    ts = tasks(kind, l)
    n = len(ts)
    return dict(scores=n, s_max=n, s_nm=n, s_exp=n, s_rinv=n, s_norm=n, s_tr=n, s_pt=n, s_pv=n, s_hi=n, s_lo=n,
                s_tab=sum(t[3] is not None for t in ts))


def norm_counts():
    return dict(sq=KT, ss=KT, y0=1, newton=3, norm_u=KT, norm_v=KT, norm_hi=KT, norm_lo=KT)


MERGE_COUNTS = dict(sub_gemm=3 * KT, br_copy=NBR * KT, gate_sig=NBR * KT, gate_mul=NBR * KT,
                    gate_add=(NBR - 1) * KT, y_hi=KT, y_lo=KT)


def up_counts(w, n):
    return dict(up_lin=2 * n, up_tap=(2 * len(segs(w)) - 1) * 2 * n, up_conv=2 * n, up_act=n, up_mul=n, up_hi=n,
                up_lo=n)


def hybrid_backbone_kernel(nc, x_in, cc_in, cb_in, w_ada, w_mod, w_all, par, sg_gain, sg_ws, sg_bs, bias_na, mask_na,
                           adab_in, mats_in, rope_in, out):
    x_spill = nc.dram_tensor("x_spill", (P, KT * T), F32, kind="Internal").ap()
    es = ExitStack()
    with es:
        def sb(name, shape, dt=F32):
            return es.enter_context(nc.sbuf_tensor(name, shape, dt))

        def sem(name):
            return es.enter_context(nc.semaphore(name))

        XY = sb("XY", [P, KT * T])
        H_hi, H_lo = sb("H_hi", [P, KT, T], F32R), sb("H_lo", [P, KT, T], F32R)
        F_hi, F_lo = sb("F_hi", [P, KT, T], F32R), sb("F_lo", [P, KT, T], F32R)
        W_st = sb("W_st", [P, 2, BW])
        W_hi, W_lo = sb("W_hi", [P, 2, BW], F32R), sb("W_lo", [P, 2, BW], F32R)
        RA = sb("RA", [P, 7680])
        TM = sb("TM", [P, 5, T])
        PAR, MOD = sb("PAR", [P, N_PAR]), sb("MOD", [P, 2, ADA_T + ADA_1])
        CC, ADAB = sb("CC", [P, KT, 2]), sb("ADAB", [P, DEPTH * ADA_T])
        SGG, SGW, SGB = sb("SGG", [P, 256]), sb("SGW", [P, NHEAD, P]), sb("SGB", [P, 2, P])
        MT = sb("MT", [P, 6, P])
        ROPE = sb("ROPE", [P, 4, SEQ])
        SM = sb("SM", [P, 64])
        PS = es.enter_context(nc.psum_tensor("PS", [P, 4096], F32))

        X3 = XY[:, :].rearrange("p (k t) -> p k t", k=KT)
        TAB = XY[:, 0:NHEAD * NAW].rearrange("p (h n) -> p h n", h=NHEAD)
        MASK = XY[:, NHEAD * NAW:(NHEAD + 1) * NAW]
        PB = [XY[:, 3584 + T * i:3584 + T * (i + 1)] for i in range(2)]
        PT = [XY[:, 5120:5120 + T], TM[:, 0, :]]
        SQ = [TM[:, 0, :], TM[:, 1, :]]
        Y0, RT, TT = TM[:, 2, :], TM[:, 3, :], TM[:, 4, :]

        def ra(at, a, b):
            return RA[:, at:at + a * b].rearrange("p (a b) -> p a b", a=a)

        MQ, MK, MV = ra(0, 4, T), ra(3072, 4, T), ra(6144, 6, 256)
        NQ, NK, NV = ra(0, 2, T), ra(1536, 2, T), ra(3072, 6, 256)
        GQ, GK, GV = ra(0, 2, T), ra(1536, 1, T), ra(2304, 6, P)
        SV, SU = ra(3072, 6, 256), ra(4608, 2, T)
        BR, SIG = ra(0, NBR, T), ra(3072, 2, T)
        UA, UG = ra(0, 2, T), ra(1536, 2, T)
        ADA_W = [RA[:, BW * i:BW * (i + 1)] for i in range(ADA_SLOTS)]
        TMF = TM[:, :, :].rearrange("p a t -> p (a t)")
        MOD_W = [RA[:, 4608:4608 + BW], TMF[:, 0:BW]]
        CB = [RA[:, 6656:6656 + BW], RA[:, 5632:5632 + BW]]
        MOD_P, MOD_ACC = TMF[:, BW:2 * BW], TMF[:, 2 * BW:2 * BW + 24]
        BANKS = PS[:, 0:6 * 512].rearrange("p (b n) -> p b n", b=6)

        def pair(i, w=T):
            return PS[:, 1024 * i:1024 * i + w]

        def bank(i):
            return PS[:, 512 * i:512 * i + 512]

        def colmajor(ap):
            return ap.rearrange("p (c r) -> p r c", c=GRID_W)

        def rowmajor(ap):
            return ap.rearrange("p (r c) -> p r c", c=GRID_W)

        EPSB = SM[:, 63:64]

        def hcm(f, k):
            if k < 6:
                return f[:, 4:8, :].rearrange("p a t -> p (a t)")[:, SEQ * k:SEQ * (k + 1)]
            return f[:, 0:2, :].rearrange("p a t -> p (a t)")[:, SEQ * (k - 6):SEQ * (k - 5)]

        def f_store(f, ft, o0, q0, kind):
            if kind == "na" and q0 < SEQ:
                return f[o0:o0 + HD, ft, 0:SEQ].rearrange("p (r c) -> p c r", c=GRID_W)[:, q0 // 8:q0 // 8 + 16, :]
            return f[o0:o0 + HD, ft, q0:q0 + P]

        def ps_out(j, o0, q0, kind):
            o = bank(6 + j % 2)[o0:o0 + HD, 0:P]
            return o.rearrange("p (c r) -> p c r", r=8) if kind == "na" and q0 < SEQ else o

        def operands(kind, h):
            if kind == "mla":
                return MQ[0:MLA_K, h, :], MK[0:MLA_K, h, :], MV, HD * h, HD * (h % 2), 2 + h // 2
            r = HD * (h % 2)
            if kind == "na":
                return NQ[r:r + HD, h // 2, :], NK[r:r + HD, h // 2, :], NV, HD * h, r, h // 2
            g = HD * (h // 2)
            return GQ[g:g + HD, h % 2, :], GK[g:g + HD, 0, :], GV, g, r, 6 + h // 2

        def dest(it):
            r0, r1 = it.rows
            if it.to in ("cq", "ckv"):
                return TT
            if it.to == "kr":
                return MK[r0:r1, 0, :]
            return {"mq": MQ, "mk": MK, "nq": NQ, "nk": NK, "gq": GQ, "gk": GK}[it.to][r0:r1, it.idx, :]

        S = {n: sem(n) for n in SIGNALS}
        w_loaded = [sem("w_loaded0"), sem("w_loaded1")]
        ada_loaded = [sem(f"ada_loaded{i}") for i in range(ADA_SLOTS)]
        mod_loaded = [sem("mod_loaded0"), sem("mod_loaded1")]
        cb_loaded = [sem("cb_loaded_latent"), sem("cb_loaded_context")]
        block = es.enter_context(nc.Block())

        def wait(eng, name, value):
            if not isinstance(value, int) or value > 0:
                eng.wait_ge(S[name], value)

        def begin(eng, n, *others):
            for o in others:
                wait(eng, "phase_" + o, n)

        def end(eng, me):
            eng.drain().then_inc(S["phase_" + me], 1)

        def repeat(eng, n, body, peel_last=False):
            body(0, peel_last and n == 1)
            if n - peel_last > 1:
                with eng.Fori(1, n - peel_last) as i:
                    body(i, False)
            if peel_last and n > 1:
                body(n - 1, True)

        @block.sync
        def _(sp):
            def load(b, slot, first=False):
                if not first:
                    sp.wait_ge(S["w_hi"], b - 1)
                    sp.wait_ge(S["w_lo"], b - 1)
                sp.dma_start(W_st[:, slot, :], w_all[bass.ds(b, 1), :, :].rearrange("a p n -> (a p) n")
                             ).then_inc(w_loaded[slot], 16)

            sp.dma_start(CC[:, :, :], cc_in).then_inc(S["cc_loaded"], 16)
            for j in range(ADA_1):
                if j >= ADA_SLOTS:
                    sp.wait_ge(S["ada_used"], j - ADA_SLOTS + 1)
                sp.dma_start(ADA_W[j % ADA_SLOTS], w_ada[j]).then_inc(ada_loaded[j % ADA_SLOTS], 16)
                if j == 3:
                    sp.dma_start(XY[:, :], x_in).then_inc(S["x_loaded"], 16)
            load(0, 0, first=True)
            load(1, 1, first=True)
            with sp.Fori(1, N_BLOCKS // 2) as i:
                for u in range(2):
                    load(i * 2 + u, u)
            sp.wait_ge(S["phase_dve"], PHASES * DEPTH)
            sp.dma_start(out, X3[:, :, 0:SEQ]).then_inc(S["out_stored"], 16)
            sp.wait_ge(S["out_stored"], 16)

        @block.gpsimd
        def _(pool):
            def load_mod(q, j):
                pool.dma_start(MOD_W[q], w_mod[bass.ds(j, 1), :, :].rearrange("a p n -> (a p) n")
                               ).then_inc(mod_loaded[q], 16)

            def modulation(l):
                n, streams = mod_tiles(l)
                for q in range(2):
                    load_mod(q, ADA_1 + ADA_T * l + q)
                with pool.Fori(1, n // 2) as i:
                    for q in range(2):
                        pool.wait_ge(S["mod_acc"], i * (2 * streams) + (2 * ADA_T * l + streams * (q - 1)))
                        load_mod(q, i * 2 + (ADA_1 + ADA_T * l + q))

            pool.dma_start(ADAB[:, :], adab_in).then_inc(S["adab_loaded"], 16)
            pool.dma_start(PAR[:, :], par[0]).then_inc(S["par_loaded"], 16)
            pool.dma_start(MT[:, :, :], mats_in).then_inc(S["const_loaded"], 16)
            pool.dma_start(ROPE[:, :, :], rope_in).then_inc(S["const_loaded"], 16)
            for l in range(DEPTH):
                p0 = PHASES * l
                if l:
                    begin(pool, p0, "pe", "act", "dve")
                    pool.dma_start(PAR[:, :], par[l]).then_inc(S["par_loaded"], 16)
                    pool.dma_start(x_spill, XY[:, :]).then_inc(S["x_spilled"], 16)
                pool.dma_start(SGG[:, :], sg_gain[l]).then_inc(S["sg_loaded"], 16)
                pool.dma_start(SGW[:, :, :], sg_ws[l]).then_inc(S["sg_loaded"], 16)
                pool.dma_start(SGB[:, :, :], sg_bs[l]).then_inc(S["sg_loaded"], 16)
                if l:
                    pool.wait_ge(S["x_spilled"], 16)
                begin(pool, p0 + PH_NORM1 + 1, "act", "dve")
                pool.dma_start(TAB, bias_na[l]).then_inc(S["bias_loaded"], 16)
                pool.dma_start(MASK, mask_na).then_inc(S["mask_loaded"], 16)
                begin(pool, p0 + PH_NA, "pe", "act", "dve")
                pool.dma_start(CB[0], cb_in[0]).then_inc(cb_loaded[0], 16)
                begin(pool, p0 + PH_MERGE, "pe", "act", "dve")
                if l < DEPTH - 1:
                    pool.dma_start(CB[1], cb_in[1]).then_inc(cb_loaded[1], 16)
                modulation(l)
                begin(pool, p0 + PH_MERGE + 1, "act", "dve")
                pool.dma_start(XY[:, :], x_in if l == 0 else x_spill).then_inc(S["x_reloaded"], 16)

        @block.tensor
        def _(pe):
            base = Base()
            done = [0]

            def mm(o, lhsT, rhs, start, stop):
                return nc.tensor.matmul(o, lhsT, rhs, start=start, stop=stop)

            def have_block(b):
                pe.wait_ge(S["w_hi"], b + 1)
                pe.wait_ge(S["w_lo"], b + 1)

            def gemm(pi, w, slot, terms):
                n = len(terms)
                for k, (c, r, m, hi, lo) in enumerate(terms):
                    for q, (x, y) in enumerate(((W_hi, hi), (W_hi, lo), (W_lo, hi))):
                        for s0, sn in segs(w):
                            ins = mm(pair(pi)[0:m, s0:s0 + sn], x[0:r, slot, c:c + m], y[0:r, s0:s0 + sn],
                                     k == 0 and q == 0, k == n - 1 and q == 2)
                return ins

            def f_terms(cols, first, rows=(P, P), m=P):
                return [(c, rows[k % 2], m, F_hi[:, first + k, :], F_lo[:, first + k, :]) for k, c in enumerate(cols)]

            H_TERMS = [(P * k, P, P, H_hi[:, k, :], H_lo[:, k, :]) for k in range(KT)]

            def ada_tile(o, w):
                for k in range(KT):
                    ins = mm(o, w[:, P * k:P * k + P], CC[:, k, :], k == 0, k == KT - 1)
                return ins

            def ada():
                pe.wait_ge(S["silu_c"], 1)
                for j in range(ADA_1):
                    pe.wait_ge(ada_loaded[j % ADA_SLOTS], 16 * (j // ADA_SLOTS + 1))
                    ada_tile(PS[:, 2 * j:2 * j + 2], ADA_W[j % ADA_SLOTS]).then_inc(S["ada_used"], 1)

            def norm(ph, w):
                begin(pe, ph, "act", "dve")
                for k in range(KT):
                    pe.wait_ge(S["sq"], base["sq"] + k + 1)
                    for s0, sn in segs(w):
                        ins = mm(pair(3)[:, s0:s0 + sn], MT[:, M_ONE, :], SQ[k % 2][:, s0:s0 + sn],
                                 k == 0, k == KT - 1)
                    ins.then_inc(S["ss"], 1)
                base.advance(**norm_counts())

            def statistic(its, i):
                it = its[i]
                c = sum(len(x.src) for x in its[:i])
                pe.wait_ge(S["sq"], base["sq"] + c + len(it.src))
                wait(pe, "newton", base["newton"] + 3 * i)
                o0, o1 = it.rows
                for s0, sn in segs(it.w):
                    for q, (_, r0, r1, mat) in enumerate(it.src):
                        ins = mm(pair(3)[o0:o1, s0:s0 + sn], MT[r0:r1, mat, o0:o1],
                                 SQ[(c + q) % 2][r0:r1, s0:s0 + sn], q == 0, q == len(it.src) - 1)
                ins.then_inc(S["ss"], 1)

            def in_phase(kind, l, ph):
                begin(pe, ph, "act", "dve")
                its, b0 = items(kind, l), done[0]
                widths = tile_widths(kind, l)
                for what, t in events(kind):
                    if what == "stat":
                        statistic(its, t)
                        continue
                    if t >= 3:
                        i = max(n for n, x in enumerate(its) if any(s[0] == t - 3 for s in x.src))
                        pe.wait_ge(S["in_zn"], base["in_zn"] + sum(x.z for x in its[:i + 1]))
                    bk, is_last = block_of(kind, t)
                    slot = (b0 + bk) % 2
                    have_block(b0 + bk)
                    if kind == "mla" and t >= 8:
                        pe.wait_ge(S["in_lo"], base["in_lo"] + 4)
                        terms = f_terms([HD * (t - 8), 256 + HD * (t - 8)], 6, (P, HD), HD)
                    elif kind == "mla" and t >= 4:
                        pe.wait_ge(S["in_lo"], base["in_lo"] + 2)
                        terms = f_terms([256 * (t - 4), 256 * (t - 4) + P], 4)
                    else:
                        terms = H_TERMS
                    gemm(t % 3, widths[t], slot, terms).then_inc(S["block_done" if is_last else "sub_gemm"], 1)
                if kind == "na":
                    pe.wait_ge(S["h_perm"], base["h_perm"] + 2 * KT)
                pe.wait_ge(S["in_zn"], base["in_zn"] + sum(x.z for x in its))
                if kind == "mla":
                    first, n_blocks, kg, nv, x_hi, x_lo = 5, 1, 2, 256, F_hi, F_lo
                elif kind == "na":
                    first, n_blocks, kg, nv, x_hi, x_lo = 4, 2, 4, 256, H_hi, H_lo
                else:
                    first, n_blocks, kg, nv, x_hi, x_lo = 3, 4, 2, 384, H_hi, H_lo
                for g in range(n_blocks):
                    b = b0 + first + g
                    have_block(b)
                    for tb in range(T // P):
                        for kk in range(kg):
                            k = g * kg + kk
                            r, c, kf = P, nv * kk, k
                            if kind == "mla":
                                r, c, kf = (P, HD)[k], 512 + 256 * k, 6 + k
                            if kind == "na" and tb < SEQ // P:
                                th, tl = (hcm(f, k)[:, P * tb:P * tb + P] for f in (F_hi, F_lo))
                            else:
                                th, tl = (x[0:r, kf, P * tb:P * tb + P] for x in (x_hi, x_lo))
                            wh, wl = (x[0:r, b % 2, c:c + nv] for x in (W_hi, W_lo))
                            last = k == kg * n_blocks - 1
                            mm(bank(tb)[:, 0:nv], th, wh, k == 0, False)
                            mm(bank(tb)[:, 0:nv], tl, wh, False, False)
                            ins = mm(bank(tb)[:, 0:nv], th, wl, False, last)
                    ins.then_inc(S["block_done"], 1)
                done[0] = b0 + first + n_blocks
                if kind == "gs":
                    pe.wait_ge(S["tok_copy"], base["tok_copy"] + 2)
                    for t in range(2):
                        b = done[0]
                        have_block(b)
                        gemm(t, width(l), b % 2, H_TERMS).then_inc(S["block_done"], 1)
                        done[0] += 1
                base.advance(**in_counts(kind, l))

            def attention(kind, l, ph):
                begin(pe, ph, "act", "dve")
                ts = tasks(kind, l)

                def scores(j):
                    h, q0, keys, _ = ts[j]
                    wait(pe, "s_exp", base["s_exp"] + j - 1 if j >= 2 else 0)
                    q, k, *_ = operands(kind, h)
                    c = 0
                    for k0, n in keys:
                        a = 0
                        while a < n:
                            m = min(n - a, 512 - (c + a) % 512)
                            ins = mm(pair(j % 2)[:, c + a:c + a + m], q[:, q0:q0 + P], k[:, k0 + a:k0 + a + m],
                                     True, True)
                            a += m
                        c += n
                    ins.then_inc(S["scores"], 1)

                def transposes(j):
                    pe.wait_ge(S["s_norm"], base["s_norm"] + j + 1)
                    wait(pe, "s_pt", base["s_pt"] + j)
                    for t in range(sum(n for _, n in ts[j][2]) // P):
                        ins = nc.tensor.transpose(pair(2)[:, P * t:P * t + P], PB[j % 2][:, P * t:P * t + P],
                                                  MT[:, M_ID, :])
                    ins.then_inc(S["s_tr"], 1)

                def values(j):
                    h, q0, keys, _ = ts[j]
                    pe.wait_ge(S["s_pt"], base["s_pt"] + j + 1)
                    wait(pe, "s_lo", base["s_lo"] + j - 1 if j >= 2 else 0)
                    _, _, v, c, o0, _ = operands(kind, h)
                    kts = [(k0 + a) // P for k0, n in keys for a in range(0, n, P)]
                    for t, kt in enumerate(kts):
                        ins = mm(bank(6 + j % 2)[o0:o0 + HD, 0:P], v[:, kt, c:c + HD], PT[j % 2][:, P * t:P * t + P],
                                 t == 0, t == len(kts) - 1)
                    ins.then_inc(S["s_pv"], 1)

                scores(0)
                scores(1)
                transposes(0)
                for j in range(len(ts)):
                    if j + 2 < len(ts):
                        scores(j + 2)
                    if j + 1 < len(ts):
                        transposes(j + 1)
                    values(j)
                base.advance(**att_counts(kind, l))

            def gating(l, ph):
                begin(pe, ph, "act", "dve")
                n_ch = width(l) // P
                pe.wait_ge(S["sg_vn"], base["sg_vn"] + n_ch)
                for g in range(2):
                    for n in range(n_ch):
                        for e in range(2):
                            gg = 2 * g + e
                            ins = mm(pair(g)[HD * e:HD * e + HD, P * n:P * n + P], SV[:, n, HD * gg:HD * gg + HD],
                                     SGW[:, gg, :], True, True)
                    ins.then_inc(S["sg_mix"], 1)
                base.advance(sg_vn=n_ch, sg_mix=2)

            def merge(l, ph):
                begin(pe, ph, "act", "dve")
                w, b0 = width(l), done[0]

                def body(i, _):
                    for u in range(2):
                        b = b0 + (NBR + 1) * u
                        have_block(i * 10 + b)
                        for r in range(NBR):
                            wait(pe, "br_copy", i * 8 + (base["br_copy"] + NBR * u + r - 1))
                            gemm(2 + r % 2, w, b % 2, f_terms([256 * r, 256 * r + P], 2 * r)).then_inc(
                                S["sub_gemm" if r < NBR - 1 else "block_done"], 1)
                        for r in range(NBR):
                            b += 1
                            have_block(i * 10 + b)
                            wait(pe, "gate_sig", i * 8 + (base["gate_sig"] + NBR * u + r - 1))
                            gemm(r % 2, w, b % 2, H_TERMS).then_inc(S["block_done"], 1)

                repeat(pe, KT // 2, body)
                done[0] += B_MERGE
                base.advance(**MERGE_COUNTS)

            def out_tiles(w, k_tiles, free):
                b0 = done[0]

                def body(i, _):
                    for u in range(2):
                        have_block(i * 2 + (b0 + u))
                        wait(pe, free, i * 2 + (base[free] + u - 1))
                        gemm(u, w, (b0 + u) % 2, f_terms([P * k for k in range(k_tiles)], 0)).then_inc(
                            S["block_done"], 1)

                repeat(pe, KT // 2, body)
                done[0] += KT
                base.advance(**{free: KT})

            def ffn(l, ph):
                w = width(l)
                for g, n in enumerate(GROUPS):
                    begin(pe, ph + 2 * g, "act", "dve")
                    b0 = done[0]

                    def body(i, _):
                        for u in range(4):
                            have_block(i * 4 + (b0 + u))
                            wait(pe, "up_conv", i * 4 + (base["up_conv"] + u - 3))
                            gemm(u, w, (b0 + u) % 2, H_TERMS).then_inc(S["block_done"], 1)

                    repeat(pe, n // 2, body)
                    done[0] += 2 * n
                    base.advance(**up_counts(w, n))
                    end(pe, "pe")
                    begin(pe, ph + 2 * g + 1, "act", "dve")
                    out_tiles(w, n, "down_add")
                    end(pe, "pe")

            pe.wait_ge(S["const_loaded"], 32)
            for l in range(DEPTH):
                p0, w = PHASES * l, width(l)
                if l == 0:
                    ada()
                end(pe, "pe")
                norm(p0 + PH_NORM1, T)
                end(pe, "pe")
                for kind, ph in (("mla", PH_MLA), ("na", PH_NA), ("gs", PH_GS)):
                    in_phase(kind, l, p0 + ph)
                    end(pe, "pe")
                    attention(kind, l, p0 + ph + 1)
                    end(pe, "pe")
                pe.wait_ge(S["sg_loaded"], 48 * (l + 1))
                gating(l, p0 + PH_SG)
                end(pe, "pe")
                merge(l, p0 + PH_MERGE)
                end(pe, "pe")
                begin(pe, p0 + PH_OUT, "act", "dve")
                out_tiles(w, KT, "out_add")
                end(pe, "pe")
                norm(p0 + PH_NORM2, w)
                end(pe, "pe")
                ffn(l, p0 + PH_FFN)

        @block.scalar
        def _(act):
            base = Base()
            done = [0]

            def op(o, i, func, **kw):
                return nc.scalar.activation(o, i, func, **kw)

            def split_hi(b, slot, n_loads):
                act.wait_ge(w_loaded[slot], n_loads)
                op(W_hi[:, slot, :], W_st[:, slot, :], ACT.Copy).then_inc(S["w_hi"], 1)

            def used(i, per, b, stop=False):
                act.wait_ge(S["block_done"], i * per + (b + 1))
                if not stop:
                    split_hi(None, b % 2, i * (8 * per) + 16 * ((b + 2) // 2 + 1))

            def norm(ph, w, sc, sh):
                begin(act, ph, "pe", "dve")
                for k in range(KT):
                    if k >= 2:
                        act.wait_ge(S["ss"], base["ss"] + k - 1)
                    op(SQ[k % 2][:, 0:w], X3[:, k, 0:w], ACT.Square).then_inc(S["sq"], 1)
                act.wait_ge(S["ss"], base["ss"] + KT)
                op(Y0[:, 0:w], pair(3, w), ACT.Abs_reciprocal_sqrt, bias=EPSB).then_inc(S["y0"], 1)
                act.wait_ge(S["newton"], base["newton"] + 3)
                for k in range(KT):
                    v = (Y0, TT)[k % 2]
                    act.wait_ge(S["norm_u"], base["norm_u"] + k + 1)
                    if k >= 2:
                        act.wait_ge(S["norm_lo"], base["norm_lo"] + k - 1)
                    for c, (s0, sn) in enumerate(segs(w)):
                        ins = op(v[:, s0:s0 + sn], SQ[k % 2][:, s0:s0 + sn], ACT.Identity,
                                 scale=MOD[:, c, sc + k:sc + k + 1], bias=MOD[:, c, sh + k:sh + k + 1])
                    ins.then_inc(S["norm_v"], 1)
                    act.wait_ge(S["norm_v"], base["norm_v"] + k + 1)
                    op(H_hi[:, k, 0:w], v[:, 0:w], ACT.Copy).then_inc(S["norm_hi"], 1)
                base.advance(**norm_counts())

            def in_phase(kind, l, ph):
                begin(act, ph, "pe", "dve")
                its, b0 = items(kind, l), done[0]
                n_hi = 0
                for what, t in events(kind):
                    if what == "gemm":
                        bk, is_last = block_of(kind, t)
                        if is_last:
                            used(0, 0, b0 + bk)
                        else:
                            act.wait_ge(S["sub_gemm"], base["sub_gemm"] + (t - 4 if t < 8 else t - 5) + 1)
                        for i, it in enumerate(its):
                            if it.src[-1][0] != t:
                                continue
                            c = sum(len(x.src) for x in its[:i])
                            for q, (tile, r0, r1, _) in enumerate(it.src):
                                n, before = c + q - 2, 0
                                for m, x in enumerate(its):
                                    n -= len(x.src)
                                    if n < 0:
                                        before = m + 1
                                        break
                                if c + q >= 2:
                                    act.wait_ge(S["ss"], base["ss"] + before)
                                op(SQ[(c + q) % 2][r0:r1, 0:it.w], pair(tile % 3)[r0:r1, 0:it.w], ACT.Square
                                   ).then_inc(S["sq"], 1)
                        continue
                    it = its[t]
                    r0, r1 = it.rows
                    act.wait_ge(S["ss"], base["ss"] + t + 1)
                    wait(act, "newton", base["newton"] + 3 * t)
                    op(Y0[r0:r1, 0:it.w], pair(3)[r0:r1, 0:it.w], ACT.Abs_reciprocal_sqrt, bias=EPSB[r0:r1, :]
                       ).then_inc(S["y0"], 1)
                    if it.to in ("cq", "ckv"):
                        for q, (_, s0, s1, _) in enumerate(it.src):
                            n_hi += 1
                            act.wait_ge(S["in_zn"], base["in_zn"] + n_hi)
                            op(F_hi[s0:s1, 3 + n_hi, 0:it.w], TT[s0:s1, 0:it.w], ACT.Copy).then_inc(S["in_hi"], 1)
                    if it.to == "kr":
                        act.wait_ge(S["rope_step"], base["rope_step"] + 4)
                        for h in range(1, NHEAD):
                            op(MK[r0:r1, h, :], MK[r0:r1, 0, :], ACT.Copy).then_inc(S["kr_copy"], 1)
                first, n_blocks = {"mla": (5, 1), "na": (4, 2), "gs": (3, 4)}[kind]
                for g in range(n_blocks):
                    used(0, 0, b0 + first + g)
                done[0] = b0 + first + n_blocks
                if kind == "gs":
                    op(GV[:, :, :], BANKS[:, :, 0:P], ACT.Copy).then_inc(S["tok_copy"], 1)
                    op(SV[:, :, :], BANKS[:, :, P:P + 256], ACT.Gelu_apprx_tanh).then_inc(S["tok_copy"], 1)
                    for t in range(2):
                        used(0, 0, done[0])
                        op(SU[:, t, 0:width(l)], pair(t, width(l)), ACT.Gelu_apprx_tanh).then_inc(S["sg_u"], 1)
                        done[0] += 1
                else:
                    op((MV if kind == "mla" else NV)[:, :, :], BANKS[:, :, 0:256], ACT.Copy).then_inc(S["tok_copy"], 1)
                base.advance(**in_counts(kind, l))

            def attention(kind, l, ph):
                begin(act, ph, "pe", "dve")
                ts = tasks(kind, l)
                scale = MLA_K ** -0.5 if kind == "mla" else HD ** -0.5

                def exp(j):
                    n = sum(x[1] for x in ts[j][2])
                    act.wait_ge(S["s_nm"], base["s_nm"] + j + 1)
                    if j >= 2:
                        act.wait_ge(S["s_tr"], base["s_tr"] + j - 1)
                    op(PB[j % 2][:, 0:n], pair(j % 2, n), ACT.Exp, scale=scale, bias=SM[:, 36 + j % 4:37 + j % 4],
                       accum_out=SM[:, 40 + j % 4:41 + j % 4]).then_inc(S["s_exp"], 1)

                def store_hi(j):
                    act.wait_ge(S["s_pv"], base["s_pv"] + j + 1)
                    _, _, _, _, o0, ft = operands(kind, ts[j][0])
                    q0 = ts[j][1]
                    op(f_store(F_hi, ft, o0, q0, kind), ps_out(j, o0, q0, kind), ACT.Copy).then_inc(S["s_hi"], 1)

                def copy_pt(j):
                    n = sum(x[1] for x in ts[j][2])
                    act.wait_ge(S["s_tr"], base["s_tr"] + j + 1)
                    wait(act, "s_pv", base["s_pv"] + j - 1 if j >= 2 else 0)
                    op(PT[j % 2][:, 0:n], pair(2, n), ACT.Copy).then_inc(S["s_pt"], 1)

                exp(0)
                exp(1)
                copy_pt(0)
                for j in range(len(ts)):
                    if j + 1 < len(ts):
                        copy_pt(j + 1)
                    if j + 2 < len(ts):
                        exp(j + 2)
                    store_hi(j)
                base.advance(**att_counts(kind, l))

            def gating(l, ph):
                begin(act, ph, "pe", "dve")
                n_ch = width(l) // P
                for n in range(n_ch):
                    op(TM[:, n // 3, 256 * (n % 3):256 * (n % 3) + 256], SV[:, n, :], ACT.Square, accum_out=SM[:, n:n + 1]).then_inc(S["sg_sq"], 1)
                act.wait_ge(S["sg_sq"], base["sg_sq"] + n_ch)
                op(SM[:, 8:8 + n_ch], SM[:, 0:n_ch], ACT.Abs_reciprocal_sqrt, scale=1.0 / 256, bias=EPSB
                   ).then_inc(S["sg_y0"], 1)
                w = width(l)
                for g in range(2):
                    act.wait_ge(S["sg_o"], base["sg_o"] + g + 1)
                    op(F_hi[:, 4 + g, 0:w], TM[:, 2 + g, 0:w], ACT.Copy).then_inc(S["sg_hi"], 1)
                base.advance(sg_sq=n_ch, sg_y0=1, sg_o=2, sg_hi=2)

            def merge(l, ph):
                begin(act, ph, "pe", "dve")
                w, b0 = width(l), done[0]

                def silu_c(c):
                    act.wait_ge(cb_loaded[c], 16 * (1 + l * (c == 0)))
                    op(CB[c], CB[c], ACT.Silu).then_inc(S["cb_silu"], 1)

                silu_c(0)

                def body(i, _):
                    for u in range(2):
                        b = b0 + (NBR + 1) * u
                        for r in range(NBR):
                            if r < NBR - 1:
                                act.wait_ge(S["sub_gemm"], i * 6 + (base["sub_gemm"] + 3 * u + r + 1))
                            else:
                                used(i, 10, b)
                            wait(act, "gate_mul", i * 8 + (base["gate_mul"] + NBR * (u - 1) + r + 1)
                                 if not isinstance(i, int) or u else 0)
                            op(BR[:, r, 0:w], pair(2 + r % 2, w), ACT.Copy).then_inc(S["br_copy"], 1)
                        if isinstance(i, int) and u == 0 and l < DEPTH - 1:
                            silu_c(1)
                        for r in range(NBR):
                            b += 1
                            used(i, 10, b)
                            wait(act, "gate_mul", i * 8 + (base["gate_mul"] + NBR * u + r - 1)
                                 if not isinstance(i, int) or u or r > 1 else 0)
                            op(SIG[:, r % 2, 0:w], pair(r % 2, w), ACT.Sigmoid,
                               bias=PAR[:, bass.ds(i * 2 + (u + C_BG + KT * r), 1)]).then_inc(S["gate_sig"], 1)

                repeat(act, KT // 2, body)
                done[0] += B_MERGE
                for k in range(KT):
                    act.wait_ge(S["gate_add"], base["gate_add"] + 3 * (k + 1))
                    op(F_hi[:, k, 0:w], X3[:, k, 0:w], ACT.Copy).then_inc(S["y_hi"], 1)
                base.advance(**MERGE_COUNTS)

            def out_tiles(last_phase=False):
                b0 = done[0]

                def body(i, final):
                    for u in range(2):
                        used(i, 2, b0 + u, stop=final)

                repeat(act, KT // 2, body, peel_last=last_phase)
                done[0] += KT

            def ffn(l, ph):
                w = width(l)
                for g, n in enumerate(GROUPS):
                    begin(act, ph + 2 * g, "pe", "dve")
                    b0, t0 = done[0], sum(GROUPS[:g])

                    def body(i, _):
                        for u in range(4):
                            used(i, 4, b0 + u)
                            s, gate = u // 2, u % 2
                            wait(act, "up_lo", i * 2 + (base["up_lo"] + s - 1) if not isinstance(i, int) else 0)
                            col = u // 2 + t0 + FFN_T * gate
                            op((UA, UG)[gate][:, s, 0:w], pair(u, w), ACT.Identity,
                               scale=PAR[:, bass.ds(i * 2 + (C_W1 + col), 1)],
                               bias=PAR[:, bass.ds(i * 2 + (C_CB + col), 1)]).then_inc(S["up_lin"], 1)
                            if gate:
                                act.wait_ge(S["up_conv"], i * 4 + (base["up_conv"] + u + 1))
                                op(UG[:, s, 0:w], UG[:, s, 0:w], ACT.Silu).then_inc(S["up_act"], 1)
                                act.wait_ge(S["up_mul"], i * 2 + (base["up_mul"] + s + 1))
                                op(F_hi[:, bass.ds(i * 2 + s, 1), 0:w].rearrange("p a t -> p (a t)"), UA[:, s, 0:w],
                                   ACT.Copy).then_inc(S["up_hi"], 1)

                    repeat(act, n // 2, body)
                    done[0] += 2 * n
                    base.advance(**up_counts(w, n))
                    end(act, "act")
                    begin(act, ph + 2 * g + 1, "pe", "dve")
                    out_tiles(l == DEPTH - 1 and g == len(GROUPS) - 1)
                    end(act, "act")

            act.wait_ge(S["cc_loaded"], 16)
            op(CC[:, :, :], CC[:, :, :], ACT.Silu).then_inc(S["silu_c"], 1)
            for b in range(2):
                split_hi(b, b, 16)
            act.wait_ge(S["const_loaded"], 32)
            act.wait_ge(S["x_loaded"], 16)
            act.wait_ge(S["phase_dve"], 1)
            for l in range(DEPTH):
                p0, w = PHASES * l, width(l)
                end(act, "act")
                norm(p0 + PH_NORM1, T, SC1 + ADA_T * l, SH1 + ADA_T * l)
                end(act, "act")
                for kind, ph in (("mla", PH_MLA), ("na", PH_NA), ("gs", PH_GS)):
                    in_phase(kind, l, p0 + ph)
                    end(act, "act")
                    attention(kind, l, p0 + ph + 1)
                    end(act, "act")
                gating(l, p0 + PH_SG)
                end(act, "act")
                merge(l, p0 + PH_MERGE)
                end(act, "act")
                begin(act, p0 + PH_OUT, "pe", "dve")
                out_tiles()
                end(act, "act")
                norm(p0 + PH_NORM2, w, SC2, SH2)
                end(act, "act")
                ffn(l, p0 + PH_FFN)

        @block.vector
        def _(dve):
            base = Base()
            done = [0]

            def tt(o, a, b, f):
                return nc.vector.tensor_tensor(o, a, b, f)

            def stt(o, a, s, b, f0, f1):
                return nc.vector.scalar_tensor_tensor(o, a, s, b, f0, f1)

            def sub(o, a, hi):
                return tt(o, a, hi.bitcast(F32), ALU.subtract)

            def split_lo(slot, n_hi):
                dve.wait_ge(S["w_hi"], n_hi)
                sub(W_lo[:, slot, :], W_st[:, slot, :], W_hi[:, slot, :]).then_inc(S["w_lo"], 1)

            def used(i, per, b, stop=False):
                dve.wait_ge(S["block_done"], i * per + (b + 1))
                if not stop:
                    split_lo(b % 2, i * per + (b + 3))

            def newton(r0, r1, w, n, ss):
                m, y, t = pair(3)[r0:r1, 0:w], Y0[r0:r1, 0:w], RT[r0:r1, 0:w]
                b = base["newton"] + 3 * n
                dve.wait_ge(S["y0"], base["y0"] + n + 1)
                dve.wait_ge(S["ss"], ss)
                stt(t, m, EPS, y, ALU.add, ALU.mult).then_inc(S["newton"], 1)
                dve.wait_ge(S["newton"], b + 1)
                stt(t, t, -0.5, y, ALU.mult, ALU.mult).then_inc(S["newton"], 1)
                dve.wait_ge(S["newton"], b + 2)
                stt(t, t, 1.5, y, ALU.add, ALU.mult).then_inc(S["newton"], 1)
                dve.wait_ge(S["newton"], b + 3)

            n_mod = [0]

            def one_plus_scale(c):
                nc.vector.tensor_scalar_add(MOD[:, :, c:c + KT], MOD[:, :, c:c + KT], 1.0).then_inc(S["mod_step"], 1)
                n_mod[0] += 1
                dve.wait_ge(S["mod_step"], n_mod[0])

            def ada():
                dve.wait_ge(S["adab_loaded"], 16)
                dve.wait_ge(S["ada_used"], ADA_1)
                v = PS[:, 0:2 * ADA_1].rearrange("p (j c) -> p c j", c=2)
                for c in range(2):
                    tt(MOD[:, c, 0:ADA_1], v[:, c, :], ADAB[:, 0:ADA_1], ALU.add).then_inc(S["mod_step"], 1)
                n_mod[0] += 2
                dve.wait_ge(S["mod_step"], n_mod[0])

            def norm(ph, w):
                begin(dve, ph, "pe", "act")
                newton(0, P, w, 0, base["ss"] + KT)

                def lo(k):
                    dve.wait_ge(S["norm_hi"], base["norm_hi"] + k + 1)
                    sub(H_lo[:, k, 0:w], (Y0, TT)[k % 2][:, 0:w], H_hi[:, k, 0:w]).then_inc(S["norm_lo"], 1)

                for k in range(KT):
                    wait(dve, "norm_v", base["norm_v"] + k - 1 if k >= 2 else 0)
                    tt(SQ[k % 2][:, 0:w], X3[:, k, 0:w], RT[:, 0:w], ALU.mult).then_inc(S["norm_u"], 1)
                    if k:
                        lo(k - 1)
                lo(KT - 1)
                base.advance(**norm_counts())

            def in_phase(kind, l, ph):
                begin(dve, ph, "pe", "act")
                its, b0 = items(kind, l), done[0]
                z = n_lo = n_rope = 0
                for what, t in events(kind):
                    if what == "gemm":
                        bk, is_last = block_of(kind, t)
                        if is_last:
                            used(0, 0, b0 + bk)
                        else:
                            dve.wait_ge(S["sub_gemm"], base["sub_gemm"] + (t - 4 if t < 8 else t - 5) + 1)
                        if kind == "na":
                            for k in (2 * t, 2 * t + 1):
                                for f, x in ((F_hi, H_hi), (F_lo, H_lo)):
                                    nc.vector.tensor_copy(colmajor(hcm(f, k)), rowmajor(x[:, k, 0:SEQ].bitcast(F32))
                                                          ).then_inc(S["h_perm"], 1)
                        continue
                    it = its[t]
                    r0, r1 = it.rows
                    wait(dve, "in_zn", base["in_zn"] + z)
                    newton(r0, r1, it.w, t, base["ss"] + t + 1)
                    for q, (tile, s0, s1, _) in enumerate(it.src):
                        src, d = pair(tile % 3), dest(it)
                        gain = PAR[s0:s1, it.gain + q:it.gain + q + 1]
                        if it.to in ("cq", "ckv"):
                            wait(dve, "in_lo", base["in_lo"] + n_lo)
                            stt(TT[s0:s1, 0:it.w], src[s0:s1, 0:it.w], gain, RT[s0:s1, 0:it.w], ALU.mult, ALU.mult
                                ).then_inc(S["in_zn"], 1)
                            z += 1
                            n_lo += 1
                            dve.wait_ge(S["in_hi"], base["in_hi"] + n_lo)
                            sub(F_lo[s0:s1, 3 + n_lo, 0:it.w], TT[s0:s1, 0:it.w], F_hi[s0:s1, 3 + n_lo, 0:it.w]
                                ).then_inc(S["in_lo"], 1)
                        elif kind == "na":
                            stt(colmajor(d[:, 0:SEQ]), rowmajor(src[r0:r1, 0:SEQ]), gain, rowmajor(RT[r0:r1, 0:SEQ]),
                                ALU.mult, ALU.mult).then_inc(S["in_zn"], 1)
                            if it.w == T:
                                stt(d[:, SEQ:T], src[r0:r1, SEQ:T], gain, RT[r0:r1, SEQ:T], ALU.mult, ALU.mult
                                    ).then_inc(S["in_zn"], 1)
                            z += it.z
                        else:
                            stt(d[:, 0:it.w], src[r0:r1, 0:it.w], gain, RT[r0:r1, 0:it.w], ALU.mult, ALU.mult
                                ).then_inc(S["in_zn"], 1)
                            z += 1
                    if it.rope is not None:
                        dve.wait_ge(S["in_zn"], base["in_zn"] + z)
                        if it.to == "mq":
                            d, r0, r1 = MQ[64:96, it.idx, :], 64, 96
                        dl, s = d[:, 0:SEQ], TT[r0:r1, 0:SEQ]
                        n = base["rope_step"] + 4 * n_rope
                        wait(dve, "in_lo", base["in_lo"] + n_lo)
                        nc.vector.stream_shuffle(s, dl, ROT_MLA if it.rope else ROT_GQA).then_inc(S["rope_step"], 1)
                        dve.wait_ge(S["rope_step"], n + 1)
                        tt(s, s, ROPE[r0:r1, it.rope + 1, :], ALU.mult).then_inc(S["rope_step"], 1)
                        tt(dl, dl, ROPE[r0:r1, it.rope, :], ALU.mult).then_inc(S["rope_step"], 1)
                        dve.wait_ge(S["rope_step"], n + 3)
                        tt(dl, dl, s, ALU.add).then_inc(S["rope_step"], 1)
                        dve.wait_ge(S["rope_step"], n + 4)
                        n_rope += 1
                if kind == "mla":
                    dve.wait_ge(S["bias_loaded"], 16 * (l + 1))
                    dve.wait_ge(S["mask_loaded"], 16 * (l + 1))
                    for h in range(NHEAD):
                        tt(TAB[:, h, :], TAB[:, h, :], MASK, ALU.add).then_inc(S["mask_step"], 1)
                    dve.wait_ge(S["mask_step"], NHEAD * (l + 1))

                first, n_blocks = {"mla": (5, 1), "na": (4, 2), "gs": (3, 6)}[kind]
                for g in range(n_blocks):
                    used(0, 0, b0 + first + g)
                done[0] = b0 + first + n_blocks
                base.advance(**in_counts(kind, l))

            def attention(kind, l, ph):
                begin(dve, ph, "pe", "act")
                ts = tasks(kind, l)
                scale = MLA_K ** -0.5 if kind == "mla" else HD ** -0.5
                n_tab = [0]
                def maximum(j):
                    h, _, keys, tc = ts[j]
                    n = sum(x[1] for x in keys)
                    dve.wait_ge(S["scores"], base["scores"] + j + 1)
                    if tc is not None:
                        m, n_tab[0] = keys[0][1], n_tab[0] + 1
                        stt(pair(j % 2, m), TAB[:, h, tc:tc + m], 1.0 / scale, pair(j % 2, m), ALU.mult, ALU.add
                            ).then_inc(S["s_tab"], 1)
                        dve.wait_ge(S["s_tab"], base["s_tab"] + n_tab[0])
                    nc.vector.reduce_max(SM[:, 32 + j % 4:33 + j % 4], pair(j % 2, n), AX.X).then_inc(S["s_max"], 1)
                    dve.wait_ge(S["s_max"], base["s_max"] + j + 1)
                    nc.vector.tensor_scalar_mul(SM[:, 36 + j % 4:37 + j % 4], SM[:, 32 + j % 4:33 + j % 4], -scale
                                                ).then_inc(S["s_nm"], 1)

                def store_lo(j):
                    dve.wait_ge(S["s_hi"], base["s_hi"] + j + 1)
                    _, _, _, _, o0, ft = operands(kind, ts[j][0])
                    q0 = ts[j][1]
                    sub(f_store(F_lo, ft, o0, q0, kind), ps_out(j, o0, q0, kind), f_store(F_hi, ft, o0, q0, kind)
                        ).then_inc(S["s_lo"], 1)

                def normalise(j):
                    n = sum(x[1] for x in ts[j][2])
                    dve.wait_ge(S["s_exp"], base["s_exp"] + j + 1)
                    r = SM[:, 44 + j % 4:45 + j % 4]
                    nc.vector.reciprocal(r, SM[:, 40 + j % 4:41 + j % 4]).then_inc(S["s_rinv"], 1)
                    dve.wait_ge(S["s_rinv"], base["s_rinv"] + j + 1)
                    nc.vector.tensor_scalar_mul(PB[j % 2][:, 0:n], PB[j % 2][:, 0:n], r).then_inc(S["s_norm"], 1)

                maximum(0)
                maximum(1)
                normalise(0)
                for j in range(len(ts)):
                    if j + 1 < len(ts):
                        normalise(j + 1)
                    if j + 2 < len(ts):
                        maximum(j + 2)
                    if j:
                        store_lo(j - 1)
                store_lo(len(ts) - 1)
                base.advance(**att_counts(kind, l))

            def gating(l, ph):
                begin(dve, ph, "pe", "act")
                w, n_ch = width(l), width(l) // P
                c = [base["sg_step"]]
                ms, y, t = SM[:, 0:n_ch], SM[:, 8:8 + n_ch], SM[:, 16:16 + n_ch]

                def step(ins):
                    ins.then_inc(S["sg_step"], 1)
                    c[0] += 1
                    dve.wait_ge(S["sg_step"], c[0])

                dve.wait_ge(S["sg_loaded"], 48 * (l + 1))
                dve.wait_ge(S["sg_y0"], base["sg_y0"] + 1)
                step(nc.vector.tensor_scalar(ms, ms, 1.0 / 256, EPS, ALU.mult, ALU.add))
                step(tt(t, ms, y, ALU.mult))
                step(stt(t, t, -0.5, y, ALU.mult, ALU.mult))
                step(stt(t, t, 1.5, y, ALU.add, ALU.mult))
                for n in range(n_ch):
                    stt(SV[:, n, :], SV[:, n, :], SM[:, 16 + n:17 + n], SGG[:, :], ALU.mult, ALU.mult
                        ).then_inc(S["sg_vn"], 1)
                for g in range(2):
                    dve.wait_ge(S["sg_mix"], base["sg_mix"] + g + 1)
                    o = TM[:, 2 + g, 0:w]
                    step(tt(o.rearrange("p (n q) -> p n q", q=P), pair(g, w).rearrange("p (n q) -> p n q", q=P),
                            SGB[:, g:g + 1, :].to_broadcast([P, n_ch, P]), ALU.add))
                    tt(o, o, SU[:, g, 0:w], ALU.mult).then_inc(S["sg_o"], 1)
                for g in range(2):
                    dve.wait_ge(S["sg_hi"], base["sg_hi"] + g + 1)
                    sub(F_lo[:, 4 + g, 0:w], TM[:, 2 + g, 0:w], F_hi[:, 4 + g, 0:w]).then_inc(S["sg_lo"], 1)
                base.advance(sg_step=c[0] - base["sg_step"], sg_y0=1, sg_vn=n_ch, sg_mix=2, sg_o=2, sg_hi=2, sg_lo=2)

            def merge(l, ph):
                begin(dve, ph, "pe", "act")
                w, b0 = width(l), done[0]
                n_mod_tiles, streams = mod_tiles(l)
                per = 2 * n_mod_tiles // KT

                def mod_tile(i, s):
                    dve.wait_ge(mod_loaded[s % 2], i * (8 * per) + (8 * ADA_T * l + 16 * (s // 2 + 1)))
                    for c in range(streams):
                        if isinstance(i, int) and s == 0:
                            dve.wait_ge(S["cb_silu"], 2 * l + c + 1)
                        wait(dve, "mod_acc", i * (per * streams) + (2 * ADA_T * l + streams * s + c))
                        if s == 0:
                            wait(dve, "mod_fold", i * streams + KT * l)
                        k = per * c + s
                        nc.vector.tensor_tensor_reduce(MOD_P, MOD_W[s % 2], CB[c], 1.0, 0.0, ALU.mult, ALU.add,
                                                       MOD_ACC[:, k:k + 1]).then_inc(S["mod_acc"], 1)

                def fold(i):
                    dve.wait_ge(S["mod_acc"], i * (per * streams) + (2 * ADA_T * l + streams * per))
                    for c in range(streams):
                        tt(MOD[:, c, bass.ds(i * per + ADA_1, per)], MOD_ACC[:, per * c:per * (c + 1)],
                           ADAB[:, bass.ds(i * per + (ADA_T * l + ADA_1), per)], ALU.add).then_inc(S["mod_fold"], 1)

                def body(i, _):
                    for u in range(2):
                        b = b0 + (NBR + 1) * u
                        y = XY[:, bass.ds(i * (2 * T) + u * T, w)]
                        used(i, 10, b)
                        for s in range(NBR, per // 2):
                            mod_tile(i, u * (per // 2) + s - NBR)
                        for r in range(NBR):
                            b += 1
                            used(i, 10, b)
                            dve.wait_ge(S["gate_sig"], i * 8 + (base["gate_sig"] + NBR * u + r + 1))
                            dve.wait_ge(S["br_copy"], i * 8 + (base["br_copy"] + NBR * u + r + 1))
                            t = TM[:, 3 + r % 2, 0:w] if r else y
                            tt(t, SIG[:, r % 2, 0:w], BR[:, r, 0:w], ALU.mult).then_inc(S["gate_mul"], 1)
                            if r:
                                dve.wait_ge(S["gate_mul"], i * 8 + (base["gate_mul"] + NBR * u + r + 1))
                                if r > 1:
                                    dve.wait_ge(S["gate_add"], i * 6 + (base["gate_add"] + 3 * u + r - 1))
                                tt(y, y, t, ALU.add).then_inc(S["gate_add"], 1)
                            mod_tile(i, (u + 1) * (per // 2) - NBR + r)
                    fold(i)

                repeat(dve, KT // 2, body)
                done[0] += B_MERGE
                dve.wait_ge(S["mod_fold"], KT * l + KT // 2 * streams)
                one_plus_scale(SC2)
                for k in range(KT):
                    dve.wait_ge(S["y_hi"], base["y_hi"] + k + 1)
                    sub(F_lo[:, k, 0:w], X3[:, k, 0:w], F_hi[:, k, 0:w]).then_inc(S["y_lo"], 1)
                base.advance(**MERGE_COUNTS)

            def out_tiles(w, gate, name, last_phase=False):
                b0 = done[0]

                def body(i, final):
                    for u in range(2):
                        used(i, 2, b0 + u, stop=final)
                        for c, (s0, sn) in enumerate(segs(w)):
                            x = XY[:, bass.ds(i * (2 * T) + (u * T + s0), sn)]
                            ins = stt(x, pair(u)[:, s0:s0 + sn], MOD[:, c, bass.ds(i * 2 + (gate + u), 1)], x,
                                      ALU.mult, ALU.add)
                        ins.then_inc(S[name], 1)

                repeat(dve, KT // 2, body, peel_last=last_phase)
                done[0] += KT
                base.advance(**{name: KT})

            def ffn(l, ph):
                w = width(l)
                taps = 2 * len(segs(w)) - 1
                for g, n in enumerate(GROUPS):
                    begin(dve, ph + 2 * g, "pe", "act")
                    b0, t0 = done[0], sum(GROUPS[:g])

                    def body(i, _):
                        for u in range(4):
                            used(i, 4, b0 + u)
                            s, gate = u // 2, u % 2
                            col = u // 2 + t0 + FFN_T * gate
                            o, ps = (UA, UG)[gate][:, s, :], pair(u)
                            dve.wait_ge(S["up_lin"], i * 4 + (base["up_lin"] + u + 1))
                            k = 0
                            for s0, sn in segs(w):
                                e = s0 + sn
                                for cw, oo, ii in ((C_W0, (s0 + 1, e), (s0, e - 1)), (C_W2, (s0, e - 1), (s0 + 1, e))):
                                    ins = stt(o[:, oo[0]:oo[1]], ps[:, ii[0]:ii[1]],
                                              PAR[:, bass.ds(i * 2 + (cw + col), 1)], o[:, oo[0]:oo[1]],
                                              ALU.mult, ALU.add)
                                    k += 1
                                    if k <= taps:
                                        ins.then_inc(S["up_tap"], 1)
                                        dve.wait_ge(S["up_tap"], i * (4 * taps) + (base["up_tap"] + taps * u + k))
                            ins.then_inc(S["up_conv"], 1)
                            if gate:
                                dve.wait_ge(S["up_conv"], i * 4 + (base["up_conv"] + u + 1))
                                dve.wait_ge(S["up_act"], i * 2 + (base["up_act"] + s + 1))
                                tt(UA[:, s, 0:w], UA[:, s, 0:w], UG[:, s, 0:w], ALU.mult).then_inc(S["up_mul"], 1)
                                dve.wait_ge(S["up_mul"], i * 2 + (base["up_mul"] + s + 1))
                                dve.wait_ge(S["up_hi"], i * 2 + (base["up_hi"] + s + 1))
                                fl, fh = (f[:, bass.ds(i * 2 + s, 1), 0:w].rearrange("p a t -> p (a t)")
                                          for f in (F_lo, F_hi))
                                sub(fl, UA[:, s, 0:w], fh).then_inc(S["up_lo"], 1)

                    repeat(dve, n // 2, body)
                    done[0] += 2 * n
                    base.advance(**up_counts(w, n))
                    end(dve, "dve")
                    begin(dve, ph + 2 * g + 1, "pe", "act")
                    out_tiles(w, G2, "down_add", l == DEPTH - 1 and g == len(GROUPS) - 1)
                    end(dve, "dve")

            nc.vector.memset(EPSB, EPS)
            for b in range(2):
                dve.wait_ge(w_loaded[b], 16)
                split_lo(b, b + 1)
            for l in range(DEPTH):
                p0, w = PHASES * l, width(l)
                if l == 0:
                    ada()
                one_plus_scale(SC1 + ADA_T * l)
                dve.wait_ge(S["par_loaded"], 16 * (l + 1))
                end(dve, "dve")
                norm(p0 + PH_NORM1, T)
                end(dve, "dve")
                for kind, ph in (("mla", PH_MLA), ("na", PH_NA), ("gs", PH_GS)):
                    in_phase(kind, l, p0 + ph)
                    end(dve, "dve")
                    attention(kind, l, p0 + ph + 1)
                    end(dve, "dve")
                gating(l, p0 + PH_SG)
                end(dve, "dve")
                merge(l, p0 + PH_MERGE)
                end(dve, "dve")
                begin(dve, p0 + PH_OUT, "pe", "act")
                dve.wait_ge(S["x_reloaded"], 16 * (l + 1))
                out_tiles(w, G1, "out_add")
                end(dve, "dve")
                norm(p0 + PH_NORM2, w)
                end(dve, "dve")
                ffn(l, p0 + PH_FFN)


def kernel(**inputs):
    import numpy as np
    import concourse.bacc as bacc
    from concourse.bass_utils import run_bass_kernel_spmd

    a = {k: np.asarray(v) for k, v in inputs.items()}
    f = np.float32

    def feat(v):
        return v.reshape(-1, P, v.shape[-1]).transpose(1, 0, 2)

    def pad_rows(v, n):
        return np.concatenate([v, np.zeros((n - v.shape[0],) + v.shape[1:], f)], 0)

    def col_tile(w):
        return feat(w).reshape(P, -1)

    def fill(w):
        return np.concatenate([w, np.zeros((P, BW - w.shape[1]), f)], 1)

    x_in = np.concatenate([feat(a["x"][0].T), feat(a["ctx"][0].T)], 2).reshape(P, KT * T)
    cc_in = np.stack([feat(a["c"].T)[..., 0], feat(a["c_ctx"][:, None])[..., 0]], 2)
    w_ada = np.stack([col_tile(a["w_ada"][0][:, P * j:P * j + P]) for j in range(ADA_1)])
    w_mod = np.concatenate([a["w_ada"][l].T.reshape(ADA_T, P, D) for l in range(DEPTH)])
    cb_in = np.stack([np.tile(a["c"], (P, 1)), np.tile(a["c_ctx"], (P, 1))])
    adab_in = np.concatenate([a["b_ada"][l].reshape(-1, P).T for l in range(DEPTH)], 1)
    blocks, pars, sgg, sgw, sgb, bias = [], [], [], [], [], []
    o_mla, o_sg, o_gqa = 768, 768 + 480, 768 + 480 + 512
    qc, qr = np.arange(P) // 8, np.arange(P) % 8
    kc, kr = np.arange(384) // 8, np.arange(384) % 8
    dr = kr[None, :] - qr[:, None] + 7

    def window(query0, key0, n):
        q, k = query0 + qc[:, None], key0 + kc[None, :n]
        start = np.clip(q - 8, 0, GRID_W - 16)
        ok = (k >= start) & (k < start + 16)
        return np.clip(k - q + 15, 0, 30), np.where(ok, 0.0, -1e30).astype(f)

    wins = [window(0, 0, 256), window(16, 0, 384), window(48, 32, 256)]
    mask_na = np.concatenate([m for _, m in wins], 1)
    for l in range(DEPTH):
        wi = a["w_in"][l]
        cols = lambda c, n=P: wi[:, c:c + n]
        gq = wi[:, o_gqa:o_gqa + 256].reshape(D, 2, 2, HD)
        ckv1 = np.concatenate([cols(o_mla + 384, 64), cols(o_mla + 448, 32), np.zeros((D, 32), f)], 1)
        b = [col_tile(cols(o_mla)), col_tile(cols(o_mla + P)), col_tile(cols(o_mla + 256)), col_tile(ckv1)]
        uq = a["mla_w_uq"][l].reshape(256, NHEAD, MLA_K)
        uq = np.concatenate([uq, np.zeros((256, NHEAD, P - MLA_K), f)], 2)
        b.append(np.concatenate([col_tile(uq[:, h]) for h in range(NHEAD)], 1))
        ukv = pad_rows(a["mla_w_ukv"][l], 256).reshape(256, NHEAD, 2, HD)
        b.append(np.concatenate([feat(ukv[:, :, e].reshape(256, 256)).reshape(P, 512) for e in range(2)], 1))
        b += [col_tile(cols(P * t)) for t in range(4)]
        b += list(feat(wi[:, 512:768]).reshape(P, 2, BW).transpose(1, 0, 2))
        b += [col_tile(gq[:, :, r].reshape(D, P)) for r in range(2)] + [col_tile(cols(o_gqa + 256))]
        vs = np.concatenate([wi[:, o_gqa + 384:o_gqa + 512], wi[:, o_sg + 256:o_sg + 512]], 1)
        b += [fill(v) for v in feat(vs).reshape(P, 4, 768).transpose(1, 0, 2)]
        b += [col_tile(cols(o_sg + P * t)) for t in range(2)]
        for m in range(KT):
            c = slice(P * m, P * m + P)
            b.append(np.concatenate([col_tile(a["w_branch"][l, i][:, c]) for i in range(NBR)], 1))
            b += [col_tile(a["w_gate"][l, i][:, c]) for i in range(NBR)]
        b += [col_tile(a["w_out"][l][:, P * m:P * m + P]) for m in range(KT)]
        t0 = 0
        for n in GROUPS:
            for t in range(t0, t0 + n):
                for e in range(2):
                    c = P * (t + FFN_T * e)
                    b.append(col_tile(a["w_up"][l][:, c:c + P]))
            b += [fill(col_tile(a["w_down"][l][P * t0:P * (t0 + n), P * m:P * m + P])) for m in range(KT)]
            t0 += n
        blocks += b
        ft = lambda v: v.reshape(-1, P).T
        pr = np.zeros((P, N_PAR), f)
        for c, name in ((C_NAQ, "na_q_norm"), (C_NAK, "na_k_norm"), (C_GQ, "gqa_q_norm"), (C_GK, "gqa_k_norm")):
            pr[:, c] = np.tile(a[name][l], 2)
        pr[:MLA_K, C_MQ], pr[:MLA_K, C_MK] = a["mla_q_norm"][l], a["mla_k_norm"][l]
        pr[:, C_CQ:C_CQ + 2] = ft(a["mla_cq_norm"][l])
        pr[:, C_CKV:C_CKV + 2] = ft(pad_rows(a["mla_ckv_norm"][l], 256))
        pr[:, C_BG:C_BG + NBR * KT] = ft(a["b_gate"][l].reshape(-1))
        for i, c in enumerate((C_W0, C_W1, C_W2)):
            pr[:, c:c + 2 * FFN_T] = ft(a["conv_w"][l, i])
        pr[:, C_CB:C_CB + 2 * FFN_T] = ft(a["conv_b"][l])
        pars.append(pr)
        sgg.append(np.tile(a["sg_v_norm"][l], (P, 1)))
        sgw.append(a["sg_w_s"][l].transpose(2, 0, 1))
        sgb.append(np.repeat(a["sg_b_s"][l].reshape(2, 2, 1, P), HD, 2).reshape(2, P, P).transpose(1, 0, 2))
        rpb = a["na_rpb"][l]
        bias.append(np.concatenate([rpb[:, dr[:, :d.shape[1]], d] for d, _ in wins], 2).transpose(1, 0, 2))

    idx = np.arange(P)
    mats = np.zeros((6, P, P), f)
    mats[M_ONE], mats[M_256], mats[M_192] = 1 / D, 1 / 256, f(1 / 192)
    mats[M_64] = (idx[:, None] // HD == idx[None, :] // HD) / HD
    mats[M_MLA, :64, :64], mats[M_MLA, 64:96, 64:96] = 1 / 64, 1 / 32
    mats[M_ID] = np.eye(P)
    t = np.arange(SEQ)
    rope = np.zeros((P, 4, SEQ), f)
    for e, (first, dim, rows) in enumerate(((0, HD, P), (64, 32, 96))):
        half = dim // 4
        inv = f(10000.0) ** (-np.arange(half, dtype=f) / f(half))
        for p in range(first, rows):
            d = (p - first) % dim
            pos = (t // GRID_W if d < dim // 2 else t % GRID_W).astype(f)
            ang = pos * inv[d % half]
            sign = -1 if d % (dim // 2) < half else 1
            rope[p, 2 * e], rope[p, 2 * e + 1] = np.cos(ang), sign * np.sin(ang)

    arrays = dict(x_in=x_in, cc_in=cc_in, cb_in=cb_in, w_ada=w_ada, w_mod=w_mod, w_all=np.stack(blocks), par=np.stack(pars),
                  sg_gain=np.stack(sgg), sg_ws=np.stack(sgw), sg_bs=np.stack(sgb), bias_na=np.stack(bias),
                  mask_na=mask_na, adab_in=adab_in, mats_in=mats.transpose(1, 0, 2), rope_in=rope)
    nc = bacc.Bacc("TRN2", target_bir_lowering=False, num_devices=1)
    args = {}
    for name in arrays:
        arrays[name] = np.ascontiguousarray(arrays[name], dtype=f)
        args[name] = nc.dram_tensor(name, arrays[name].shape, F32, kind="ExternalInput").ap()
    out = nc.dram_tensor("out", (P, KT, SEQ), F32, kind="ExternalOutput").ap()
    hybrid_backbone_kernel(nc, out=out, **args)
    r = run_bass_kernel_spmd(nc, [arrays], core_ids=[0])
    return r.results[0]["out"].transpose(2, 1, 0).reshape(1, SEQ, D)
```

```python
from contextlib import ExitStack

import concourse.bass as bass
from concourse import mybir

F32 = mybir.dt.float32
F32R = mybir.dt.float32r
ALU = mybir.AluOpType
ACT = mybir.ActivationFunctionType
AX = mybir.AxisListType

P = 128
D = 1024
KT = D // P
SEQ, CTX = 512, 256
T = SEQ + CTX
DEPTH = 2
GRID_W = 64
HD = 64
NHEAD = 4
FFN_T = 22
GROUPS = (8, 8, 6)
NBR = 4
BW = KT * P
MLA_K = 96
EPS = 1e-6
NAW = 896
NA_WIN = ((0, 256, 0), (0, 384, 256), (128, 384, 256), (256, 256, 640))

B_MLA, B_NA, B_GS = 6, 6, 9
B_IN = B_MLA + B_NA + B_GS
B_MERGE = KT * (NBR + 1)
B_LAYER = B_IN + B_MERGE + KT + 2 * FFN_T + KT * len(GROUPS)
N_BLOCKS = DEPTH * B_LAYER
ADA_T = 6 * KT
ADA_1 = 2 * KT

C_NAQ, C_NAK, C_GQ, C_GK, C_MQ, C_MK, C_CQ, C_CKV, C_MK2, C_BG = 0, 1, 2, 3, 4, 5, 6, 8, 10, 11
C_W0, C_W1, C_W2, C_CB = (C_BG + NBR * KT + 2 * FFN_T * i for i in range(4))
N_PAR = C_CB + 2 * FFN_T
M_ONE, M_256, M_192, M_64, M_MLA, M_ID = range(6)
SH1, SC1, G1, SH2, SC2, G2 = (KT * i for i in range(6))

PH_ADA, PH_NORM1, PH_MLA, PH_NA, PH_GS, PH_SG, PH_MERGE, PH_OUT, PH_NORM2, PH_FFN = 0, 1, 2, 4, 6, 8, 9, 10, 11, 12
PHASES = PH_FFN + 2 * len(GROUPS)

ROT_MLA = [(i // 16) * 16 + (i + 8) % 16 for i in range(32)]
ROT_GQA = [(i + 16) % 32 for i in range(32)]

SIGNALS = """
w_hi w_lo block_done sub_gemm phase_pe phase_act phase_dve
ada_used scale_acc mod_step silu_c cc_loaded par_loaded const_loaded sg_loaded bias_loaded mask_loaded mask_step
adab_loaded cb_silu mod_acc mod_fold x_loaded sq_sum x_head x_reloaded x_spilled out_stored
sq ss y0 newton norm_u norm_v norm_hi norm_lo
y_sq in_zn in_hi in_lo h_perm rope_shuf rope_step kr_copy tok_done tok_copy
scores s_tab s_max s_nm s_exp s_rinv s_norm s_tr s_pt s_pv s_hi s_lo
sg_u sg_sq sg_y0 sg_step sg_vn sg_mix sg_add sg_o sg_hi sg_lo
br_copy gate_sig gate_mul gate_add y_hi y_lo out_add
up_lin up_tap up_conv up_act up_mul up_hi up_lo down_add""".split()


class Base:

    def __init__(self):
        self.v = {}

    def __getitem__(self, name):
        return self.v.get(name, 0)

    def advance(self, **counts):
        for name, n in counts.items():
            self.v[name] = self.v.get(name, 0) + n


def width(l):
    return T if l < DEPTH - 1 else SEQ


def mod_tiles(l):
    return (ADA_T, 2) if l < DEPTH - 1 else (ADA_T - ADA_1, 1)


def segs(w):
    return [(0, SEQ), (SEQ, CTX)] if w == T else [(0, SEQ)]


def tasks(kind, l):
    out = []
    for h in range(NHEAD):
        for j in range(SEQ // P):
            if kind == "na":
                k0, n, tc = NA_WIN[j]
                out.append((h, j * P, [(k0, n), (SEQ, CTX)], tc))
            else:
                out.append((h, j * P, [(0, SEQ), (SEQ, CTX)], None))
        if width(l) == T:
            for j in range(CTX // P):
                out.append((h, SEQ + j * P, [(SEQ, CTX)], None))
    return out


class Item:

    def __init__(self, to, src, rows, w, gain, idx=0, rope=None, z=None):
        self.to, self.src, self.rows, self.w, self.gain, self.idx, self.rope = to, src, rows, w, gain, idx, rope
        self.z = len(src) if z is None else z


def items(kind, l):
    w = width(l)
    if kind == "mla":
        return ([Item("ckv", [(0, 0, P, M_192), (1, 0, HD, M_192)], (0, P), T, C_CKV),
                 Item("kr", [(1, 64, 96, M_MLA)], (64, 96), T, C_MK, rope=2),
                 Item("cq", [(2, 0, P, M_256), (3, 0, P, M_256)], (0, P), w, C_CQ)]
                + [Item("mk", [(4 + h, 0, P, M_64)], (0, P), T, C_MK2, 2 * h, z=2) for h in range(NHEAD // 2)]
                + [Item("mq", [(6 + h, 0, P, M_MLA)], (0, P), w, C_MQ, h, rope=2) for h in range(NHEAD)])
    if kind == "na":
        return ([Item("nq", [(t, 0, P, M_64)], (0, P), w, C_NAQ, t, z=len(segs(w))) for t in range(2)]
                + [Item("nk", [(2 + t, 0, P, M_64)], (0, P), T, C_NAK, t, z=2) for t in range(2)])
    return ([Item("gq", [(t, 0, P, M_64)], (0, P), w, C_GQ, t, rope=0) for t in range(2)]
            + [Item("gk", [(2, 0, P, M_64)], (0, P), T, C_GK, 0, rope=0)])


def tile_widths(kind, l):
    w = width(l)
    return {"mla": [T, T, w, w] + [T] * 2 + [w] * 4, "na": [w, w, T, T], "gs": [w, w, T]}[kind]


def events(kind):
    g, s = (lambda t: ("gemm", t)), (lambda i: ("stat", i))
    if kind == "mla":
        return [g(0), g(1), s(0), g(2), s(1), g(3), g(4), s(2), s(3), g(5), g(6), s(4), g(7), s(5), g(8), s(6),
                g(9), s(7), s(8)]
    if kind == "na":
        return [g(0), g(1), s(0), g(2), s(1), g(3), s(2), s(3)]
    return [g(0), g(1), s(0), g(2), s(1), s(2)]


def block_of(kind, t):
    if kind == "mla" and t >= 4:
        return (5, False) if t < 6 else (4, t == 9)
    return t, True


def in_counts(kind, l):
    its = items(kind, l)
    n_rope = sum(i.rope is not None for i in its)
    return dict(sq=sum(len(i.src) for i in its), ss=len(its), y0=len(its), y_sq=len(its), newton=2 * len(its),
                in_zn=sum(i.z for i in its), in_hi=4 * (kind == "mla"), in_lo=4 * (kind == "mla"),
                rope_shuf=n_rope, rope_step=3 * n_rope, kr_copy=3 * (kind == "mla"),
                sub_gemm=5 * (kind == "mla"), h_perm=2 * KT * (kind == "na"), tok_copy=2 if kind == "gs" else 1, sg_u=2 * (kind == "gs"))


def att_counts(kind, l):
    ts = tasks(kind, l)
    n = len(ts)
    return dict(scores=n, s_max=n, s_nm=n, s_exp=n, s_rinv=n, s_norm=n, s_tr=n, s_pt=n, s_pv=n, s_hi=n, s_lo=n,
                s_tab=sum(t[3] is not None for t in ts))


def norm_counts(own_squares):
    return dict(sq=KT, ss=KT if own_squares else 1, y0=1, y_sq=1, newton=2, norm_u=KT, norm_v=KT, norm_hi=KT, norm_lo=KT)


MERGE_COUNTS = dict(sub_gemm=3 * KT, br_copy=NBR * KT, gate_sig=NBR * KT, gate_mul=NBR * KT,
                    gate_add=(NBR - 1) * KT, y_hi=KT, y_lo=KT)


def up_counts(w, n):
    return dict(up_lin=2 * n, up_tap=(2 * len(segs(w)) - 1) * 2 * n, up_conv=2 * n, up_act=n, up_mul=n, up_hi=n,
                up_lo=n)


def hybrid_backbone_kernel(nc, x_in, cc_in, cb_in, w_ada, w_mod, w_all, par, sg_gain, sg_ws, sg_bs, bias_na, mask_na,
                           adab_in, mats_in, rope_in, out):
    x_spill = nc.dram_tensor("x_spill", (P, KT * T), F32, kind="Internal").ap()
    es = ExitStack()
    with es:
        def sb(name, shape, dt=F32):
            return es.enter_context(nc.sbuf_tensor(name, shape, dt))

        def sem(name):
            return es.enter_context(nc.semaphore(name))

        XY = sb("XY", [P, KT * T])
        H_hi, H_lo = sb("H_hi", [P, KT, T], F32R), sb("H_lo", [P, KT, T], F32R)
        F_hi, F_lo = sb("F_hi", [P, KT, T], F32R), sb("F_lo", [P, KT, T], F32R)
        W_st = sb("W_st", [P, 2, BW])
        W_hi, W_lo = sb("W_hi", [P, 2, BW], F32R), sb("W_lo", [P, 2, BW], F32R)
        RA = sb("RA", [P, 7680])
        TM = sb("TM", [P, 5, T])
        PAR, MOD = sb("PAR", [P, N_PAR]), sb("MOD", [P, 2, ADA_T + ADA_1])
        CC, ADAB = sb("CC", [P, KT, 2]), sb("ADAB", [P, DEPTH * ADA_T])
        SGG, SGW, SGB = sb("SGG", [P, 256]), sb("SGW", [P, NHEAD, P]), sb("SGB", [P, 2, P])
        MT = sb("MT", [P, 6, P])
        ROPE = sb("ROPE", [P, 4, SEQ])
        SM = sb("SM", [P, 64])
        PS = es.enter_context(nc.psum_tensor("PS", [P, 4096], F32))

        X3 = XY[:, :].rearrange("p (k t) -> p k t", k=KT)
        TAB = XY[:, 0:NHEAD * NAW].rearrange("p (h n) -> p h n", h=NHEAD)
        MASK = XY[:, NHEAD * NAW:(NHEAD + 1) * NAW]
        PB = [XY[:, 3584 + T * i:3584 + T * (i + 1)] for i in range(2)]
        PT = [XY[:, 5120:5120 + T], TM[:, 0, :]]
        SQ = [TM[:, 0, :], TM[:, 1, :]]
        Y0 = [TM[:, 2, :], XY[:, 4480:4480 + T]]
        RT = [TM[:, 3, :], XY[:, 4480 + T:4480 + 2 * T]]
        TT = TM[:, 4, :]

        def ra(at, a, b):
            return RA[:, at:at + a * b].rearrange("p (a b) -> p a b", a=a)

        MQ, MK, MV = ra(0, 4, T), ra(3072, 4, T), ra(6144, 6, 256)
        NQ, NK, NV = ra(0, 2, T), ra(1536, 2, T), ra(3072, 6, 256)
        GQ, GK, GV = ra(0, 2, T), ra(1536, 1, T), ra(2304, 6, P)
        SV, SU = ra(3072, 6, 256), ra(4608, 2, T)
        BR, SIG = ra(0, NBR, T), ra(3072, 2, T)
        UA, UG = ra(0, 2, T), ra(1536, 2, T)
        SHIFT_W = [RA[:, BW * i:BW * (i + 1)] for i in range(2)]
        SCALE_W, SCALE_P = [RA[:, 2560:2560 + BW], RA[:, 4608:4608 + BW]], RA[:, 2560 + BW:2560 + 2 * BW]
        TMF = TM[:, :, :].rearrange("p a t -> p (a t)")
        MOD_W = [RA[:, 4608:4608 + BW], TMF[:, 0:BW]]
        CB = [RA[:, 6656:6656 + BW], RA[:, 5632:5632 + BW]]
        MOD_P, MOD_ACC = TMF[:, BW:2 * BW], TMF[:, 2 * BW:2 * BW + 24]
        BANKS = PS[:, 0:6 * 512].rearrange("p (b n) -> p b n", b=6)

        def pair(i, w=T):
            return PS[:, 1024 * i:1024 * i + w]

        def bank(i):
            return PS[:, 512 * i:512 * i + 512]

        def colmajor(ap):
            return ap.rearrange("p (c r) -> p r c", c=GRID_W)

        def rowmajor(ap):
            return ap.rearrange("p (r c) -> p r c", c=GRID_W)

        EPSB = SM[:, 63:64]

        def hcm(f, k):
            if k < 6:
                return f[:, 4:8, :].rearrange("p a t -> p (a t)")[:, SEQ * k:SEQ * (k + 1)]
            return f[:, 0:2, :].rearrange("p a t -> p (a t)")[:, SEQ * (k - 6):SEQ * (k - 5)]

        def f_store(f, ft, o0, q0, kind):
            if kind == "na" and q0 < SEQ:
                return f[o0:o0 + HD, ft, 0:SEQ].rearrange("p (r c) -> p c r", c=GRID_W)[:, q0 // 8:q0 // 8 + 16, :]
            return f[o0:o0 + HD, ft, q0:q0 + P]

        def ps_out(j, o0, q0, kind):
            o = bank(6 + j % 2)[o0:o0 + HD, 0:P]
            return o.rearrange("p (c r) -> p c r", r=8) if kind == "na" and q0 < SEQ else o

        def operands(kind, h):
            if kind == "mla":
                return MQ[0:MLA_K, h, :], MK[0:MLA_K, h, :], MV, HD * h, HD * (h % 2), 2 + h // 2
            r = HD * (h % 2)
            if kind == "na":
                return NQ[r:r + HD, h // 2, :], NK[r:r + HD, h // 2, :], NV, HD * h, r, h // 2
            g = HD * (h // 2)
            return GQ[g:g + HD, h % 2, :], GK[g:g + HD, 0, :], GV, g, r, 6 + h // 2

        def dest(it):
            r0, r1 = it.rows
            if it.to in ("cq", "ckv"):
                return TT
            if it.to == "kr":
                return MK[r0:r1, 0, :]
            return {"mq": MQ, "nq": NQ, "nk": NK, "gq": GQ, "gk": GK}[it.to][r0:r1, it.idx, :]

        def rope_operands(it):
            r0, r1 = (64, 96) if it.to in ("mq", "kr") else it.rows
            d = MQ[r0:r1, it.idx, :] if it.to == "mq" else dest(it)
            return d[:, 0:SEQ], TT[r0:r1, 0:SEQ]

        S = {n: sem(n) for n in SIGNALS}
        w_loaded = [sem("w_loaded0"), sem("w_loaded1")]
        shift_loaded = [sem("shift_loaded0"), sem("shift_loaded1")]
        scale_loaded = [sem("scale_loaded0"), sem("scale_loaded1")]
        mod_loaded = [sem("mod_loaded0"), sem("mod_loaded1")]
        cb_loaded = [sem("cb_loaded_latent"), sem("cb_loaded_context")]
        block = es.enter_context(nc.Block())

        def wait(eng, name, value):
            if not isinstance(value, int) or value > 0:
                eng.wait_ge(S[name], value)

        def first(i):
            return isinstance(i, int) and i == 0

        def begin(eng, n, *others):
            for o in others:
                wait(eng, "phase_" + o, n)

        def end(eng, me):
            eng.drain().then_inc(S["phase_" + me], 1)

        def repeat(eng, n, body, peel_last=False):
            body(0, peel_last and n == 1)
            if n - peel_last > 1:
                with eng.Fori(1, n - peel_last) as i:
                    body(i, False)
            if peel_last and n > 1:
                body(n - 1, True)

        @block.sync
        def _(sp):
            def load(b, slot, first=False):
                if not first:
                    sp.wait_ge(S["w_hi"], b - 1)
                    sp.wait_ge(S["w_lo"], b - 1)
                sp.dma_start(W_st[:, slot, :], w_all[bass.ds(b, 1), :, :].rearrange("a p n -> (a p) n")
                             ).then_inc(w_loaded[slot], 16)

            sp.dma_start(CC[:, :, :], cc_in).then_inc(S["cc_loaded"], 16)
            for j in range(KT):
                if j >= 2:
                    sp.wait_ge(S["scale_acc"], 2 * (j - 1))
                sp.dma_start(SCALE_W[j % 2], w_mod[SC1 + j]).then_inc(scale_loaded[j % 2], 16)
                if j >= 2:
                    sp.wait_ge(S["ada_used"], j - 1)
                sp.dma_start(SHIFT_W[j % 2], w_ada[j]).then_inc(shift_loaded[j % 2], 16)
                if j % 2:
                    k = T * (j - 1)
                    sp.dma_start(XY[:, k:k + 2 * T], x_in[:, k:k + 2 * T]).then_inc(S["x_loaded"], 16)
            load(0, 0, first=True)
            load(1, 1, first=True)
            with sp.Fori(1, N_BLOCKS // 2) as i:
                for u in range(2):
                    load(i * 2 + u, u)
            sp.wait_ge(S["phase_dve"], PHASES * DEPTH)
            sp.dma_start(out, X3[:, :, 0:SEQ]).then_inc(S["out_stored"], 16)
            sp.wait_ge(S["out_stored"], 16)

        @block.gpsimd
        def _(pool):
            done_rope = [0]

            def rotate(kind, l):
                tt = nc.gpsimd.tensor_tensor
                for it in items(kind, l):
                    if it.rope is None:
                        continue
                    n = 3 * done_rope[0]
                    done_rope[0] += 1
                    pool.wait_ge(S["rope_shuf"], done_rope[0])
                    dl, s = rope_operands(it)
                    r0, r1 = (64, 96) if it.rope else it.rows
                    tt(s, s, ROPE[r0:r1, it.rope + 1, :], ALU.mult).then_inc(S["rope_step"], 1)
                    tt(dl, dl, ROPE[r0:r1, it.rope, :], ALU.mult).then_inc(S["rope_step"], 1)
                    pool.wait_ge(S["rope_step"], n + 2)
                    tt(dl, dl, s, ALU.add).then_inc(S["rope_step"], 1)

            def load_mod(q, j):
                pool.dma_start(MOD_W[q], w_mod[bass.ds(j, 1), :, :].rearrange("a p n -> (a p) n")
                               ).then_inc(mod_loaded[q], 16)

            def modulation(l):
                n, streams = mod_tiles(l)
                for q in range(2):
                    load_mod(q, ADA_1 + ADA_T * l + q)
                with pool.Fori(1, n // 2) as i:
                    for q in range(2):
                        pool.wait_ge(S["mod_acc"], i * (2 * streams) + (2 * ADA_T * l + streams * (q - 1)))
                        load_mod(q, i * 2 + (ADA_1 + ADA_T * l + q))

            for c in range(2):
                pool.dma_start(CB[c], cb_in[c]).then_inc(cb_loaded[c], 16)
            pool.dma_start(ADAB[:, :], adab_in).then_inc(S["adab_loaded"], 16)
            pool.dma_start(PAR[:, :], par[0]).then_inc(S["par_loaded"], 16)
            pool.dma_start(MT[:, :, :], mats_in).then_inc(S["const_loaded"], 16)
            pool.dma_start(ROPE[:, :, :], rope_in).then_inc(S["const_loaded"], 16)
            for l in range(DEPTH):
                p0 = PHASES * l
                if l:
                    begin(pool, p0, "pe", "act", "dve")
                    pool.dma_start(PAR[:, :], par[l]).then_inc(S["par_loaded"], 16)
                    pool.dma_start(x_spill, XY[:, :]).then_inc(S["x_spilled"], 16)
                pool.dma_start(SGG[:, :], sg_gain[l]).then_inc(S["sg_loaded"], 16)
                pool.dma_start(SGW[:, :, :], sg_ws[l]).then_inc(S["sg_loaded"], 16)
                pool.dma_start(SGB[:, :, :], sg_bs[l]).then_inc(S["sg_loaded"], 16)
                if l:
                    pool.wait_ge(S["x_spilled"], 16)
                begin(pool, p0 + PH_NORM1 + 1, "act", "dve")
                pool.dma_start(TAB, bias_na[l]).then_inc(S["bias_loaded"], 16)
                pool.dma_start(MASK, mask_na).then_inc(S["mask_loaded"], 16)
                pool.wait_ge(S["const_loaded"], 32)
                rotate("mla", l)
                begin(pool, p0 + PH_NA, "pe", "act", "dve")
                pool.dma_start(CB[0], cb_in[0]).then_inc(cb_loaded[0], 16)
                rotate("gs", l)
                begin(pool, p0 + PH_MERGE, "pe", "act", "dve")
                if l < DEPTH - 1:
                    pool.dma_start(CB[1], cb_in[1]).then_inc(cb_loaded[1], 16)
                modulation(l)
                x3 = (x_in if l == 0 else x_spill).rearrange("p (k t) -> p k t", k=KT)
                w = width(l)
                pool.wait_ge(S["y_lo"], KT * (l + 1) - 1)
                pool.dma_start(X3[:, 0:KT - 1, 0:w], x3[:, 0:KT - 1, 0:w]).then_inc(S["x_head"], 16)
                begin(pool, p0 + PH_MERGE + 1, "act", "dve")
                pool.dma_start(X3[:, KT - 1, 0:w], x3[:, KT - 1, 0:w]).then_inc(S["x_reloaded"], 16)

        @block.tensor
        def _(pe):
            base = Base()
            done = [0]

            def mm(o, lhsT, rhs, start, stop):
                return nc.tensor.matmul(o, lhsT, rhs, start=start, stop=stop)

            def have_block(b):
                pe.wait_ge(S["w_hi"], b + 1)
                pe.wait_ge(S["w_lo"], b + 1)

            def gemm(pi, w, slot, terms):
                n = len(terms)
                for k, (c, r, m, hi, lo) in enumerate(terms):
                    for q, (x, y) in enumerate(((W_hi, hi), (W_hi, lo), (W_lo, hi))):
                        for s0, sn in segs(w):
                            ins = mm(pair(pi)[0:m, s0:s0 + sn], x[0:r, slot, c:c + m], y[0:r, s0:s0 + sn],
                                     k == 0 and q == 0, k == n - 1 and q == 2)
                return ins

            def gemm_k(pi, w, slot, k, n, hi, lo):
                for q, (x, y) in enumerate(((W_hi, hi), (W_hi, lo), (W_lo, hi))):
                    for s0, sn in segs(w):
                        ins = mm(pair(pi)[:, s0:s0 + sn], x[:, slot, P * k:P * k + P], y[:, k, s0:s0 + sn],
                                 k == 0 and q == 0, k == n - 1 and q == 2)
                return ins

            def two_early_tiles(widths, b):
                n_hi, n_lo = base["norm_hi"] - KT, base["norm_lo"] - KT
                for k in range(KT):
                    for t in range(2):
                        if k == 0:
                            have_block(b + t)
                        if t == 0:
                            pe.wait_ge(S["norm_hi"], n_hi + k + 1)
                            pe.wait_ge(S["norm_lo"], n_lo + k + 1)
                        ins = gemm_k(t, widths[t], (b + t) % 2, k, KT, H_hi, H_lo)
                        if k == KT - 1:
                            ins.then_inc(S["block_done"], 1)

            def f_terms(cols, first, rows=(P, P), m=P):
                return [(c, rows[k % 2], m, F_hi[:, first + k, :], F_lo[:, first + k, :]) for k, c in enumerate(cols)]

            H_TERMS = [(P * k, P, P, H_hi[:, k, :], H_lo[:, k, :]) for k in range(KT)]

            def ada_tile(o, w):
                for k in range(KT):
                    ins = mm(o, w[:, P * k:P * k + P], CC[:, k, :], k == 0, k == KT - 1)
                return ins

            def ada():
                pe.wait_ge(S["silu_c"], 1)
                for j in range(KT):
                    pe.wait_ge(shift_loaded[j % 2], 16 * (j // 2 + 1))
                    ada_tile(PS[:, 2 * j:2 * j + 2], SHIFT_W[j % 2]).then_inc(S["ada_used"], 1)

            def norm(ph, w, own_squares=False):
                if not own_squares:
                    begin(pe, ph, "act", "dve")
                    pe.wait_ge(S["sq_sum"], base["sq_sum"] + KT - 1)
                    for s0, sn in segs(w):
                        ins = mm(pair(3)[:, s0:s0 + sn], MT[:, M_ONE, :], TT[:, s0:s0 + sn], True, True)
                    ins.then_inc(S["ss"], 1)
                    base.advance(sq_sum=KT - 1)
                    base.advance(**norm_counts(False))
                    return
                for k in range(KT):
                    pe.wait_ge(S["sq"], base["sq"] + k + 1)
                    for s0, sn in segs(w):
                        ins = mm(pair(3)[:, s0:s0 + sn], MT[:, M_ONE, :], SQ[k % 2][:, s0:s0 + sn],
                                 k == 0, k == KT - 1)
                    ins.then_inc(S["ss"], 1)
                base.advance(**norm_counts(True))

            def statistic(its, i):
                it = its[i]
                c = sum(len(x.src) for x in its[:i])
                pe.wait_ge(S["sq"], base["sq"] + c + len(it.src))
                wait(pe, "newton", base["newton"] + 2 * i - 1 if i else 0)
                o0, o1 = it.rows
                for s0, sn in segs(it.w):
                    for q, (_, r0, r1, mat) in enumerate(it.src):
                        ins = mm(pair(3)[o0:o1, s0:s0 + sn], MT[r0:r1, mat, o0:o1],
                                 SQ[(c + q) % 2][r0:r1, s0:s0 + sn], q == 0, q == len(it.src) - 1)
                ins.then_inc(S["ss"], 1)

            def in_phase(kind, l, ph):
                its, b0 = items(kind, l), done[0]
                widths = tile_widths(kind, l)
                early = 0
                if kind == "mla":
                    two_early_tiles(widths, b0)
                    early = 2
                begin(pe, ph, "act", "dve")
                for what, t in events(kind)[early:]:
                    if what == "stat":
                        statistic(its, t)
                        continue
                    if t >= 3:
                        i = max(n for n, x in enumerate(its) if any(s[0] == t - 3 for s in x.src))
                        pe.wait_ge(S["in_zn"], base["in_zn"] + sum(x.z for x in its[:i + 1]))
                    bk, is_last = block_of(kind, t)
                    slot = (b0 + bk) % 2
                    have_block(b0 + bk)
                    if kind == "mla" and t >= 6:
                        pe.wait_ge(S["in_lo"], base["in_lo"] + 4)
                        terms = f_terms([256 * (t - 6), 256 * (t - 6) + P], 6)
                    elif kind == "mla" and t >= 4:
                        pe.wait_ge(S["in_lo"], base["in_lo"] + 2)
                        terms = f_terms([P * (t - 4), 256 + P * (t - 4)], 4, (P, HD))
                    else:
                        terms = H_TERMS
                    gemm(t % 3, widths[t], slot, terms).then_inc(S["block_done" if is_last else "sub_gemm"], 1)
                if kind == "na":
                    pe.wait_ge(S["h_perm"], base["h_perm"] + 2 * KT)
                p_last, order = {}, []
                for t in range(len(widths)):
                    p_last[t % 3] = t
                for p in sorted(p_last, key=lambda p: p_last[p]):
                    order += [2 * p, 2 * p + 1]
                if kind == "mla":
                    first, n_blocks, kg, nv, x_hi, x_lo = 5, 1, 2, 256, F_hi, F_lo
                elif kind == "na":
                    first, n_blocks, kg, nv, x_hi, x_lo = 4, 2, 4, 256, H_hi, H_lo
                else:
                    first, n_blocks, kg, nv, x_hi, x_lo = 3, 4, 2, 384, H_hi, H_lo
                for g in range(n_blocks):
                    b = b0 + first + g
                    have_block(b)
                    for tb in order:
                        if g == 0 and tb % 2 == 0:
                            i = max(n for n, x in enumerate(its) if any(s[0] == p_last[tb // 2] for s in x.src))
                            pe.wait_ge(S["in_zn"], base["in_zn"] + sum(x.z for x in its[:i + 1]))
                        for kk in range(kg):
                            k = g * kg + kk
                            r, c, kf = P, nv * kk, k
                            if kind == "mla":
                                r, c, kf = (P, HD)[k], 512 + 256 * k, 4 + k
                            if kind == "na" and tb < SEQ // P:
                                th, tl = (hcm(f, k)[:, P * tb:P * tb + P] for f in (F_hi, F_lo))
                            else:
                                th, tl = (x[0:r, kf, P * tb:P * tb + P] for x in (x_hi, x_lo))
                            wh, wl = (x[0:r, b % 2, c:c + nv] for x in (W_hi, W_lo))
                            last = k == kg * n_blocks - 1
                            mm(bank(tb)[:, 0:nv], th, wh, k == 0, False)
                            mm(bank(tb)[:, 0:nv], tl, wh, False, False)
                            ins = mm(bank(tb)[:, 0:nv], th, wl, False, last)
                    ins.then_inc(S["block_done"], 1)
                done[0] = b0 + first + n_blocks
                if kind == "gs":
                    pe.wait_ge(S["tok_copy"], base["tok_copy"] + 2)
                    for t in range(2):
                        b = done[0]
                        have_block(b)
                        gemm(t, width(l), b % 2, H_TERMS).then_inc(S["block_done"], 1)
                        done[0] += 1
                base.advance(**in_counts(kind, l))

            def attention(kind, l, ph):
                begin(pe, ph, "act", "dve")
                wait(pe, "rope_step", base["rope_step"])
                ts = tasks(kind, l)

                def scores(j):
                    h, q0, keys, _ = ts[j]
                    wait(pe, "s_exp", base["s_exp"] + j - 1 if j >= 2 else 0)
                    q, k, *_ = operands(kind, h)
                    c = 0
                    for k0, n in keys:
                        a = 0
                        while a < n:
                            m = min(n - a, 512 - (c + a) % 512)
                            ins = mm(pair(j % 2)[:, c + a:c + a + m], q[:, q0:q0 + P], k[:, k0 + a:k0 + a + m],
                                     True, True)
                            a += m
                        c += n
                    ins.then_inc(S["scores"], 1)

                def transposes(j):
                    pe.wait_ge(S["s_norm"], base["s_norm"] + j + 1)
                    wait(pe, "s_pt", base["s_pt"] + j)
                    for t in range(sum(n for _, n in ts[j][2]) // P):
                        ins = nc.tensor.transpose(pair(2)[:, P * t:P * t + P], PB[j % 2][:, P * t:P * t + P],
                                                  MT[:, M_ID, :])
                    ins.then_inc(S["s_tr"], 1)

                def values(j):
                    h, q0, keys, _ = ts[j]
                    pe.wait_ge(S["s_pt"], base["s_pt"] + j + 1)
                    wait(pe, "s_lo", base["s_lo"] + j - 1 if j >= 2 else 0)
                    _, _, v, c, o0, _ = operands(kind, h)
                    kts = [(k0 + a) // P for k0, n in keys for a in range(0, n, P)]
                    for t, kt in enumerate(kts):
                        ins = mm(bank(6 + j % 2)[o0:o0 + HD, 0:P], v[:, kt, c:c + HD], PT[j % 2][:, P * t:P * t + P],
                                 t == 0, t == len(kts) - 1)
                    ins.then_inc(S["s_pv"], 1)

                scores(0)
                scores(1)
                scores(2)
                transposes(0)
                for j in range(len(ts)):
                    if j + 3 < len(ts):
                        scores(j + 3)
                    if j + 1 < len(ts):
                        transposes(j + 1)
                    values(j)
                base.advance(**att_counts(kind, l))

            def gating(l, ph):
                begin(pe, ph, "act", "dve")
                n_ch = width(l) // P
                pe.wait_ge(S["sg_vn"], base["sg_vn"] + n_ch)
                for g in range(2):
                    for n in range(n_ch):
                        for e in range(2):
                            gg = 2 * g + e
                            ins = mm(pair(g)[HD * e:HD * e + HD, P * n:P * n + P], SV[:, n, HD * gg:HD * gg + HD],
                                     SGW[:, gg, :], True, True)
                    ins.then_inc(S["sg_mix"], 1)
                base.advance(sg_vn=n_ch, sg_mix=2)

            def merge(l, ph):
                begin(pe, ph, "act", "dve")
                w, b0 = width(l), done[0]

                def body(i, _):
                    for u in range(2):
                        b = b0 + (NBR + 1) * u
                        have_block(i * 10 + b)
                        for r in range(NBR):
                            wait(pe, "br_copy", i * 8 + (base["br_copy"] + NBR * u + r - 1))
                            gemm(2 + r % 2, w, b % 2, f_terms([256 * r, 256 * r + P], 2 * r)).then_inc(
                                S["sub_gemm" if r < NBR - 1 else "block_done"], 1)
                        for r in range(NBR):
                            b += 1
                            have_block(i * 10 + b)
                            wait(pe, "gate_sig", i * 8 + (base["gate_sig"] + NBR * u + r - 1))
                            gemm(r % 2, w, b % 2, H_TERMS).then_inc(S["block_done"], 1)

                repeat(pe, KT // 2, body)
                done[0] += B_MERGE
                base.advance(**MERGE_COUNTS)

            def out_tiles(ph, w, k_tiles, free, made, pair_read, n_read):
                b0 = done[0]
                have_block(b0)
                pe.wait_ge(S[pair_read], n_read)
                for k in range(k_tiles):
                    pe.wait_ge(S[made], base[made] - k_tiles + k + 1)
                    ins = gemm_k(0, w, b0 % 2, k, k_tiles, F_hi, F_lo)
                ins.then_inc(S["block_done"], 1)
                begin(pe, ph, "act", "dve")

                def body(i, _):
                    for u in range(2):
                        if first(i) and u == 0:
                            continue
                        have_block(i * 2 + (b0 + u))
                        wait(pe, free, i * 2 + (base[free] + u - 1))
                        gemm(u, w, (b0 + u) % 2, f_terms([P * k for k in range(k_tiles)], 0)).then_inc(
                            S["block_done"], 1)

                repeat(pe, KT // 2, body)
                done[0] += KT
                base.advance(**{free: KT})

            def ffn(l, ph):
                w = width(l)
                for g, n in enumerate(GROUPS):
                    b0 = done[0]
                    if g == 0:
                        two_early_tiles((w, w), b0)
                    begin(pe, ph + 2 * g, "act", "dve")

                    def body(i, _):
                        for u in range(4):
                            if first(i) and g == 0 and u < 2:
                                continue
                            have_block(i * 4 + (b0 + u))
                            wait(pe, "up_conv", i * 4 + (base["up_conv"] + u - 3))
                            gemm(u, w, (b0 + u) % 2, H_TERMS).then_inc(S["block_done"], 1)

                    repeat(pe, n // 2, body)
                    done[0] += 2 * n
                    base.advance(**up_counts(w, n))
                    end(pe, "pe")
                    out_tiles(ph + 2 * g + 1, w, n, "down_add", "up_lo", "up_conv", base["up_conv"] - 3)
                    end(pe, "pe")

            for l in range(DEPTH):
                p0, w = PHASES * l, width(l)
                if l == 0:
                    ada()
                    pe.wait_ge(S["const_loaded"], 32)
                end(pe, "pe")
                norm(p0 + PH_NORM1, T, own_squares=l == 0)
                end(pe, "pe")
                for kind, ph in (("mla", PH_MLA), ("na", PH_NA), ("gs", PH_GS)):
                    in_phase(kind, l, p0 + ph)
                    end(pe, "pe")
                    attention(kind, l, p0 + ph + 1)
                    end(pe, "pe")
                pe.wait_ge(S["sg_loaded"], 48 * (l + 1))
                gating(l, p0 + PH_SG)
                end(pe, "pe")
                merge(l, p0 + PH_MERGE)
                end(pe, "pe")
                out_tiles(p0 + PH_OUT, w, KT, "out_add", "y_lo", "gate_sig", base["gate_sig"] - 1)
                end(pe, "pe")
                norm(p0 + PH_NORM2, w)
                end(pe, "pe")
                ffn(l, p0 + PH_FFN)

        @block.scalar
        def _(act):
            base = Base()
            done = [0]

            def op(o, i, func, **kw):
                return nc.scalar.activation(o, i, func, **kw)

            def split_hi(b, slot, n_loads):
                act.wait_ge(w_loaded[slot], n_loads)
                op(W_hi[:, slot, :], W_st[:, slot, :], ACT.Copy).then_inc(S["w_hi"], 1)

            def used(i, per, b, stop=False):
                act.wait_ge(S["block_done"], i * per + (b + 1))
                if not stop:
                    split_hi(None, b % 2, i * (8 * per) + 16 * ((b + 2) // 2 + 1))

            def norm(ph, w, sc, sh, own_squares=False):
                if own_squares:
                    act.wait_ge(S["x_loaded"], 16 * (KT // 2))
                for k in range(KT if own_squares else 0):
                    if k >= 2:
                        act.wait_ge(S["ss"], base["ss"] + k - 1)
                    op(SQ[k % 2][:, 0:w], X3[:, k, 0:w], ACT.Square).then_inc(S["sq"], 1)
                if own_squares:
                    for b in range(2):
                        split_hi(b, b, 16)
                begin(act, ph, "pe", "dve")
                act.wait_ge(S["ss"], base["ss"] + (KT if own_squares else 1))
                op(Y0[0][:, 0:w], pair(3, w), ACT.Abs_reciprocal_sqrt, bias=EPSB).then_inc(S["y0"], 1)
                act.wait_ge(S["y0"], base["y0"] + 1)
                op(RT[0][:, 0:w], Y0[0][:, 0:w], ACT.Square).then_inc(S["y_sq"], 1)
                act.wait_ge(S["newton"], base["newton"] + 2)
                for k in range(KT):
                    v = (Y0[0], TT)[k % 2]
                    act.wait_ge(S["norm_u"], base["norm_u"] + k + 1)
                    if k >= 2:
                        act.wait_ge(S["norm_lo"], base["norm_lo"] + k - 1)
                    for c, (s0, sn) in enumerate(segs(w)):
                        ins = op(v[:, s0:s0 + sn], SQ[k % 2][:, s0:s0 + sn], ACT.Identity,
                                 scale=MOD[:, c, sc + k:sc + k + 1], bias=MOD[:, c, sh + k:sh + k + 1])
                    ins.then_inc(S["norm_v"], 1)
                    act.wait_ge(S["norm_v"], base["norm_v"] + k + 1)
                    op(H_hi[:, k, 0:w], v[:, 0:w], ACT.Copy).then_inc(S["norm_hi"], 1)
                base.advance(**norm_counts(own_squares))

            def in_phase(kind, l, ph):
                begin(act, ph, "pe", "dve")
                wait(act, "x_spilled", 16 * l)
                its, b0 = items(kind, l), done[0]
                n_hi = 0
                for what, t in events(kind):
                    if what == "gemm":
                        bk, is_last = block_of(kind, t)
                        if is_last:
                            used(0, 0, b0 + bk)
                        else:
                            act.wait_ge(S["sub_gemm"], base["sub_gemm"] + t - 3)
                        for i, it in enumerate(its):
                            if it.src[-1][0] != t:
                                continue
                            c = sum(len(x.src) for x in its[:i])
                            for q, (tile, r0, r1, _) in enumerate(it.src):
                                n, before = c + q - 2, 0
                                for m, x in enumerate(its):
                                    n -= len(x.src)
                                    if n < 0:
                                        before = m + 1
                                        break
                                if c + q >= 2:
                                    act.wait_ge(S["ss"], base["ss"] + before)
                                op(SQ[(c + q) % 2][r0:r1, 0:it.w], pair(tile % 3)[r0:r1, 0:it.w], ACT.Square
                                   ).then_inc(S["sq"], 1)
                        continue
                    it = its[t]
                    r0, r1 = it.rows
                    act.wait_ge(S["ss"], base["ss"] + t + 1)
                    y, r = Y0[t % 2][r0:r1, 0:it.w], RT[t % 2][r0:r1, 0:it.w]
                    wait(act, "newton", base["newton"] + 2 * (t - 1) if t >= 2 else 0)
                    op(y, pair(3)[r0:r1, 0:it.w], ACT.Abs_reciprocal_sqrt, bias=EPSB[r0:r1, :]
                       ).then_inc(S["y0"], 1)
                    act.wait_ge(S["y0"], base["y0"] + t + 1)
                    if t >= 2:
                        act.wait_ge(S["in_zn"], base["in_zn"] + sum(x.z for x in its[:t - 1]))
                    op(r, y, ACT.Square).then_inc(S["y_sq"], 1)
                    if it.to in ("cq", "ckv"):
                        for q, (_, s0, s1, _) in enumerate(it.src):
                            n_hi += 1
                            act.wait_ge(S["in_zn"], base["in_zn"] + sum(x.z for x in its[:t]) + q + 1)
                            op(F_hi[s0:s1, 3 + n_hi, 0:it.w], TT[s0:s1, 0:it.w], ACT.Copy).then_inc(S["in_hi"], 1)
                if kind == "mla":
                    act.wait_ge(S["rope_step"], base["rope_step"] + 3)
                    for h in range(1, NHEAD):
                        op(MK[64:96, h, :], MK[64:96, 0, :], ACT.Copy).then_inc(S["kr_copy"], 1)
                first, n_blocks = {"mla": (5, 1), "na": (4, 2), "gs": (3, 4)}[kind]
                for g in range(n_blocks):
                    used(0, 0, b0 + first + g)
                done[0] = b0 + first + n_blocks
                if kind == "gs":
                    op(GV[:, :, :], BANKS[:, :, 0:P], ACT.Copy).then_inc(S["tok_copy"], 1)
                    op(SV[:, :, :], BANKS[:, :, P:P + 256], ACT.Gelu_apprx_tanh).then_inc(S["tok_copy"], 1)
                    for t in range(2):
                        used(0, 0, done[0])
                        op(SU[:, t, 0:width(l)], pair(t, width(l)), ACT.Gelu_apprx_tanh).then_inc(S["sg_u"], 1)
                        done[0] += 1
                else:
                    op((MV if kind == "mla" else NV)[:, :, :], BANKS[:, :, 0:256], ACT.Copy).then_inc(S["tok_copy"], 1)
                base.advance(**in_counts(kind, l))

            def attention(kind, l, ph):
                begin(act, ph, "pe", "dve")
                ts = tasks(kind, l)
                scale = MLA_K ** -0.5 if kind == "mla" else HD ** -0.5

                def exp(j):
                    n = sum(x[1] for x in ts[j][2])
                    act.wait_ge(S["s_nm"], base["s_nm"] + j + 1)
                    if j >= 2:
                        act.wait_ge(S["s_tr"], base["s_tr"] + j - 1)
                    op(PB[j % 2][:, 0:n], pair(j % 2, n), ACT.Exp, scale=scale, bias=SM[:, 36 + j % 4:37 + j % 4],
                       accum_out=SM[:, 40 + j % 4:41 + j % 4]).then_inc(S["s_exp"], 1)

                def store_hi(j):
                    act.wait_ge(S["s_pv"], base["s_pv"] + j + 1)
                    _, _, _, _, o0, ft = operands(kind, ts[j][0])
                    q0 = ts[j][1]
                    op(f_store(F_hi, ft, o0, q0, kind), ps_out(j, o0, q0, kind), ACT.Copy).then_inc(S["s_hi"], 1)

                def copy_pt(j):
                    n = sum(x[1] for x in ts[j][2])
                    act.wait_ge(S["s_tr"], base["s_tr"] + j + 1)
                    wait(act, "s_pv", base["s_pv"] + j - 1 if j >= 2 else 0)
                    op(PT[j % 2][:, 0:n], pair(2, n), ACT.Copy).then_inc(S["s_pt"], 1)

                exp(0)
                exp(1)
                copy_pt(0)
                for j in range(len(ts)):
                    if j + 2 < len(ts):
                        exp(j + 2)
                    if j + 1 < len(ts):
                        copy_pt(j + 1)
                    store_hi(j)
                base.advance(**att_counts(kind, l))

            def gating(l, ph):
                begin(act, ph, "pe", "dve")
                n_ch = width(l) // P
                for n in range(n_ch):
                    op(TM[:, n // 3, 256 * (n % 3):256 * (n % 3) + 256], SV[:, n, :], ACT.Square, accum_out=SM[:, n:n + 1]).then_inc(S["sg_sq"], 1)
                act.wait_ge(S["sg_sq"], base["sg_sq"] + n_ch)
                op(SM[:, 8:8 + n_ch], SM[:, 0:n_ch], ACT.Abs_reciprocal_sqrt, scale=1.0 / 256, bias=EPSB
                   ).then_inc(S["sg_y0"], 1)
                w = width(l)
                for g in range(2):
                    act.wait_ge(S["sg_o"], base["sg_o"] + g + 1)
                    op(F_hi[:, 4 + g, 0:w], TM[:, 2 + g, 0:w], ACT.Copy).then_inc(S["sg_hi"], 1)
                base.advance(sg_sq=n_ch, sg_y0=1, sg_o=2, sg_hi=2)

            def merge(l, ph):
                begin(act, ph, "pe", "dve")
                w, b0 = width(l), done[0]

                def silu_c(c):
                    act.wait_ge(cb_loaded[c], 16 * (2 + l * (c == 0)))
                    op(CB[c], CB[c], ACT.Silu).then_inc(S["cb_silu"], 1)

                silu_c(0)

                def split_y(k):
                    act.wait_ge(S["gate_add"], base["gate_add"] + 3 * (k + 1))
                    op(F_hi[:, k, 0:w], X3[:, k, 0:w], ACT.Copy).then_inc(S["y_hi"], 1)

                def body(i, last):
                    for u in range(2):
                        b = b0 + (NBR + 1) * u
                        for r in range(NBR):
                            if r < NBR - 1:
                                act.wait_ge(S["sub_gemm"], i * 6 + (base["sub_gemm"] + 3 * u + r + 1))
                            else:
                                used(i, 10, b)
                            wait(act, "gate_mul", i * 8 + (base["gate_mul"] + NBR * (u - 1) + r + 1)
                                 if not first(i) or u else 0)
                            op(BR[:, r, 0:w], pair(2 + r % 2, w), ACT.Copy).then_inc(S["br_copy"], 1)
                        if first(i) and u == 0 and l < DEPTH - 1:
                            silu_c(1)
                        for r in range(NBR):
                            b += 1
                            used(i, 10, b)
                            wait(act, "gate_mul", i * 8 + (base["gate_mul"] + NBR * u + r - 1)
                                 if not first(i) or u or r > 1 else 0)
                            op(SIG[:, r % 2, 0:w], pair(r % 2, w), ACT.Sigmoid,
                               bias=PAR[:, bass.ds(i * 2 + (u + C_BG + KT * r), 1)]).then_inc(S["gate_sig"], 1)
                            if last and u == 1:
                                for k in range(2 * r, min(2 * r + 2, KT - 1)):
                                    split_y(k)

                repeat(act, KT // 2, body, peel_last=True)
                done[0] += B_MERGE
                split_y(KT - 1)
                base.advance(**MERGE_COUNTS)

            def out_tiles(w, name, last_phase=False, squares=False):
                b0 = done[0]

                def body(i, final):
                    for u in range(2):
                        used(i, 2, b0 + u, stop=final)
                        if squares:
                            act.wait_ge(S[name], i * 2 + (base[name] + u + 1))
                            wait(act, "sq_sum", 0 if first(i) else i * 2 + (base["sq_sum"] + u - 1))
                            op(SQ[u][:, 0:w], XY[:, bass.ds(i * (2 * T) + u * T, w)], ACT.Square).then_inc(S["sq"], 1)

                repeat(act, KT // 2, body, peel_last=last_phase)
                done[0] += KT
                base.advance(**{name: KT})
                if squares:
                    base.advance(sq_sum=KT - 1)

            def ffn(l, ph):
                w = width(l)
                for g, n in enumerate(GROUPS):
                    begin(act, ph + 2 * g, "pe", "dve")
                    b0, t0 = done[0], sum(GROUPS[:g])

                    def body(i, _):
                        for u in range(4):
                            used(i, 4, b0 + u)
                            s, gate = u // 2, u % 2
                            wait(act, "up_lo", i * 2 + (base["up_lo"] + s - 1) if not first(i) else 0)
                            col = u // 2 + t0 + FFN_T * gate
                            op((UA, UG)[gate][:, s, 0:w], pair(u, w), ACT.Identity,
                               scale=PAR[:, bass.ds(i * 2 + (C_W1 + col), 1)],
                               bias=PAR[:, bass.ds(i * 2 + (C_CB + col), 1)]).then_inc(S["up_lin"], 1)
                            if gate:
                                act.wait_ge(S["up_conv"], i * 4 + (base["up_conv"] + u + 1))
                                op(UG[:, s, 0:w], UG[:, s, 0:w], ACT.Silu).then_inc(S["up_act"], 1)
                                act.wait_ge(S["up_mul"], i * 2 + (base["up_mul"] + s + 1))
                                op(F_hi[:, bass.ds(i * 2 + s, 1), 0:w].rearrange("p a t -> p (a t)"), UA[:, s, 0:w],
                                   ACT.Copy).then_inc(S["up_hi"], 1)

                    repeat(act, n // 2, body)
                    done[0] += 2 * n
                    base.advance(**up_counts(w, n))
                    end(act, "act")
                    begin(act, ph + 2 * g + 1, "pe", "dve")
                    out_tiles(w, "down_add", l == DEPTH - 1 and g == len(GROUPS) - 1,
                              l < DEPTH - 1 and g == len(GROUPS) - 1)
                    end(act, "act")

            act.wait_ge(S["cc_loaded"], 16)
            op(CC[:, :, :], CC[:, :, :], ACT.Silu).then_inc(S["silu_c"], 1)
            for c in range(2):
                act.wait_ge(cb_loaded[c], 16)
                op(CB[c], CB[c], ACT.Silu).then_inc(S["cb_silu"], 1)
            for l in range(DEPTH):
                p0, w = PHASES * l, width(l)
                end(act, "act")
                norm(p0 + PH_NORM1, T, SC1 + ADA_T * l, SH1 + ADA_T * l, own_squares=l == 0)
                end(act, "act")
                for kind, ph in (("mla", PH_MLA), ("na", PH_NA), ("gs", PH_GS)):
                    in_phase(kind, l, p0 + ph)
                    end(act, "act")
                    attention(kind, l, p0 + ph + 1)
                    end(act, "act")
                gating(l, p0 + PH_SG)
                end(act, "act")
                merge(l, p0 + PH_MERGE)
                end(act, "act")
                begin(act, p0 + PH_OUT, "pe", "dve")
                out_tiles(w, "out_add", squares=True)
                end(act, "act")
                norm(p0 + PH_NORM2, w, SC2, SH2)
                end(act, "act")
                ffn(l, p0 + PH_FFN)

        @block.vector
        def _(dve):
            base = Base()
            done = [0]

            def tt(o, a, b, f):
                return nc.vector.tensor_tensor(o, a, b, f)

            def stt(o, a, s, b, f0, f1):
                return nc.vector.scalar_tensor_tensor(o, a, s, b, f0, f1)

            def sub(o, a, hi):
                return tt(o, a, hi.bitcast(F32), ALU.subtract)

            def split_lo(slot, n_hi):
                dve.wait_ge(S["w_hi"], n_hi)
                sub(W_lo[:, slot, :], W_st[:, slot, :], W_hi[:, slot, :]).then_inc(S["w_lo"], 1)

            def used(i, per, b, stop=False):
                dve.wait_ge(S["block_done"], i * per + (b + 1))
                if not stop:
                    split_lo(b % 2, i * per + (b + 3))

            def newton(r0, r1, w, n, ss):
                m, y, t = pair(3)[r0:r1, 0:w], Y0[n % 2][r0:r1, 0:w], RT[n % 2][r0:r1, 0:w]
                b = base["newton"] + 2 * n
                dve.wait_ge(S["y_sq"], base["y_sq"] + n + 1)
                dve.wait_ge(S["ss"], ss)
                stt(t, m, EPS, t, ALU.add, ALU.mult).then_inc(S["newton"], 1)
                dve.wait_ge(S["newton"], b + 1)
                stt(t, t, -3.0, y, ALU.add, ALU.mult).then_inc(S["newton"], 1)
                dve.wait_ge(S["newton"], b + 2)

            n_mod = [0]

            def one_plus_scale(c):
                m = MOD[:, :, c:c + KT]
                nc.vector.tensor_scalar(m, m, 1.0, -0.5, ALU.add, ALU.mult).then_inc(S["mod_step"], 1)
                n_mod[0] += 1
                dve.wait_ge(S["mod_step"], n_mod[0])

            def halve_gains(l):
                dve.wait_ge(S["par_loaded"], 16 * (l + 1))
                g = PAR[:, 0:C_BG]
                nc.vector.tensor_scalar_mul(g, g, -0.5).then_inc(S["mod_step"], 1)
                n_mod[0] += 1
                dve.wait_ge(S["mod_step"], n_mod[0])

            def ada():
                for j in range(KT):
                    dve.wait_ge(scale_loaded[j % 2], 16 * (j // 2 + 1))
                    for c in range(2):
                        if j == 0:
                            dve.wait_ge(S["cb_silu"], c + 1)
                        wait(dve, "scale_acc", 2 * j + c)
                        nc.vector.tensor_tensor_reduce(SCALE_P, SCALE_W[j % 2], CB[c], 1.0, 0.0, ALU.mult, ALU.add,
                                                       MOD[:, c, SC1 + j:SC1 + j + 1]).then_inc(S["scale_acc"], 1)
                dve.wait_ge(S["adab_loaded"], 16)
                dve.wait_ge(S["scale_acc"], 2 * KT)
                dve.wait_ge(S["ada_used"], KT)
                v = PS[:, 0:2 * KT].rearrange("p (j c) -> p c j", c=2)
                for c in range(2):
                    m = MOD[:, c, SC1:SC1 + KT]
                    tt(m, m, ADAB[:, SC1:SC1 + KT], ALU.add).then_inc(S["mod_step"], 1)
                    tt(MOD[:, c, SH1:SH1 + KT], v[:, c, :], ADAB[:, SH1:SH1 + KT], ALU.add
                       ).then_inc(S["mod_step"], 1)
                n_mod[0] += 4
                dve.wait_ge(S["mod_step"], n_mod[0])

            def norm(ph, w, own_squares=False):
                begin(dve, ph, "pe", "act")
                newton(0, P, w, 0, base["ss"] + (KT if own_squares else 1))

                def lo(k):
                    dve.wait_ge(S["norm_hi"], base["norm_hi"] + k + 1)
                    sub(H_lo[:, k, 0:w], (Y0[0], TT)[k % 2][:, 0:w], H_hi[:, k, 0:w]).then_inc(S["norm_lo"], 1)

                for k in range(KT):
                    wait(dve, "norm_v", base["norm_v"] + k - 1 if k >= 2 else 0)
                    tt(SQ[k % 2][:, 0:w], X3[:, k, 0:w], RT[0][:, 0:w], ALU.mult).then_inc(S["norm_u"], 1)
                    if k:
                        lo(k - 1)
                lo(KT - 1)
                base.advance(**norm_counts(own_squares))

            def in_phase(kind, l, ph):
                begin(dve, ph, "pe", "act")
                its, b0 = items(kind, l), done[0]
                z = n_lo = n_rope = 0
                for what, t in events(kind):
                    if what == "gemm":
                        bk, is_last = block_of(kind, t)
                        if is_last:
                            used(0, 0, b0 + bk)
                        else:
                            dve.wait_ge(S["sub_gemm"], base["sub_gemm"] + t - 3)
                        if kind == "na":
                            for k in (2 * t, 2 * t + 1):
                                for f, x in ((F_hi, H_hi), (F_lo, H_lo)):
                                    nc.vector.tensor_copy(colmajor(hcm(f, k)), rowmajor(x[:, k, 0:SEQ].bitcast(F32))
                                                          ).then_inc(S["h_perm"], 1)
                        continue
                    it = its[t]
                    r0, r1 = it.rows
                    rt = RT[t % 2]
                    newton(r0, r1, it.w, t, base["ss"] + t + 1)
                    for q, (tile, s0, s1, _) in enumerate(it.src):
                        src, d = pair(tile % 3), dest(it) if it.to != "mk" else None
                        gain = PAR[s0:s1, it.gain + q:it.gain + q + 1]
                        if it.to in ("cq", "ckv"):
                            wait(dve, "in_lo", base["in_lo"] + n_lo)
                            wait(dve, "rope_step", base["rope_step"] + 3 * n_rope)
                            stt(TT[s0:s1, 0:it.w], src[s0:s1, 0:it.w], gain, rt[s0:s1, 0:it.w], ALU.mult, ALU.mult
                                ).then_inc(S["in_zn"], 1)
                            z += 1
                            n_lo += 1
                            dve.wait_ge(S["in_hi"], base["in_hi"] + n_lo)
                            sub(F_lo[s0:s1, 3 + n_lo, 0:it.w], TT[s0:s1, 0:it.w], F_hi[s0:s1, 3 + n_lo, 0:it.w]
                                ).then_inc(S["in_lo"], 1)
                        elif kind == "na":
                            stt(colmajor(d[:, 0:SEQ]), rowmajor(src[r0:r1, 0:SEQ]), gain, rowmajor(rt[r0:r1, 0:SEQ]),
                                ALU.mult, ALU.mult).then_inc(S["in_zn"], 1)
                            if it.w == T:
                                stt(d[:, SEQ:T], src[r0:r1, SEQ:T], gain, rt[r0:r1, SEQ:T], ALU.mult, ALU.mult
                                    ).then_inc(S["in_zn"], 1)
                            z += it.z
                        elif it.to == "mk":
                            for h in range(2):
                                e0, e1 = HD * h, HD * (h + 1)
                                stt(MK[0:HD, it.idx + h, :], src[e0:e1, 0:T], PAR[e0:e1, it.gain:it.gain + 1],
                                    rt[e0:e1, 0:T], ALU.mult, ALU.mult).then_inc(S["in_zn"], 1)
                            z += it.z
                        else:
                            stt(d[:, 0:it.w], src[r0:r1, 0:it.w], gain, rt[r0:r1, 0:it.w], ALU.mult, ALU.mult
                                ).then_inc(S["in_zn"], 1)
                            z += 1
                    if it.rope is not None:
                        dve.wait_ge(S["in_zn"], base["in_zn"] + z)
                        dl, s = rope_operands(it)
                        wait(dve, "in_lo", base["in_lo"] + n_lo)
                        wait(dve, "rope_step", base["rope_step"] + 3 * n_rope)
                        nc.vector.stream_shuffle(s, dl, ROT_MLA if it.rope else ROT_GQA).then_inc(S["rope_shuf"], 1)
                        n_rope += 1
                if kind == "mla":
                    dve.wait_ge(S["bias_loaded"], 16 * (l + 1))
                    dve.wait_ge(S["mask_loaded"], 16 * (l + 1))
                    for h in range(NHEAD):
                        tt(TAB[:, h, :], TAB[:, h, :], MASK, ALU.add).then_inc(S["mask_step"], 1)
                    dve.wait_ge(S["mask_step"], NHEAD * (l + 1))

                first, n_blocks = {"mla": (5, 1), "na": (4, 2), "gs": (3, 6)}[kind]
                for g in range(n_blocks):
                    used(0, 0, b0 + first + g)
                done[0] = b0 + first + n_blocks
                base.advance(**in_counts(kind, l))

            def attention(kind, l, ph):
                begin(dve, ph, "pe", "act")
                ts = tasks(kind, l)
                scale = MLA_K ** -0.5 if kind == "mla" else HD ** -0.5
                n_tab = [0]
                def maximum(j):
                    h, _, keys, tc = ts[j]
                    n = sum(x[1] for x in keys)
                    dve.wait_ge(S["scores"], base["scores"] + j + 1)
                    if tc is not None:
                        m, n_tab[0] = keys[0][1], n_tab[0] + 1
                        stt(pair(j % 2, m), TAB[:, h, tc:tc + m], 1.0 / scale, pair(j % 2, m), ALU.mult, ALU.add
                            ).then_inc(S["s_tab"], 1)
                        dve.wait_ge(S["s_tab"], base["s_tab"] + n_tab[0])
                    nc.vector.reduce_max(SM[:, 32 + j % 4:33 + j % 4], pair(j % 2, n), AX.X).then_inc(S["s_max"], 1)
                    dve.wait_ge(S["s_max"], base["s_max"] + j + 1)
                    nc.vector.tensor_scalar_mul(SM[:, 36 + j % 4:37 + j % 4], SM[:, 32 + j % 4:33 + j % 4], -scale
                                                ).then_inc(S["s_nm"], 1)

                def store_lo(j):
                    dve.wait_ge(S["s_hi"], base["s_hi"] + j + 1)
                    _, _, _, _, o0, ft = operands(kind, ts[j][0])
                    q0 = ts[j][1]
                    sub(f_store(F_lo, ft, o0, q0, kind), ps_out(j, o0, q0, kind), f_store(F_hi, ft, o0, q0, kind)
                        ).then_inc(S["s_lo"], 1)

                def normalise(j):
                    n = sum(x[1] for x in ts[j][2])
                    dve.wait_ge(S["s_exp"], base["s_exp"] + j + 1)
                    r = SM[:, 44 + j % 4:45 + j % 4]
                    nc.vector.reciprocal(r, SM[:, 40 + j % 4:41 + j % 4]).then_inc(S["s_rinv"], 1)
                    dve.wait_ge(S["s_rinv"], base["s_rinv"] + j + 1)
                    nc.vector.tensor_scalar_mul(PB[j % 2][:, 0:n], PB[j % 2][:, 0:n], r).then_inc(S["s_norm"], 1)

                maximum(0)
                maximum(1)
                normalise(0)
                maximum(2)
                for j in range(len(ts)):
                    if j + 1 < len(ts):
                        normalise(j + 1)
                    if j + 3 < len(ts):
                        maximum(j + 3)
                    if j:
                        store_lo(j - 1)
                store_lo(len(ts) - 1)
                base.advance(**att_counts(kind, l))

            def gating(l, ph):
                begin(dve, ph, "pe", "act")
                w, n_ch = width(l), width(l) // P
                c = [base["sg_step"]]
                ms, y, t = SM[:, 0:n_ch], SM[:, 8:8 + n_ch], SM[:, 16:16 + n_ch]

                def step(ins):
                    ins.then_inc(S["sg_step"], 1)
                    c[0] += 1
                    dve.wait_ge(S["sg_step"], c[0])

                dve.wait_ge(S["sg_loaded"], 48 * (l + 1))
                dve.wait_ge(S["sg_y0"], base["sg_y0"] + 1)
                step(nc.vector.tensor_scalar(ms, ms, 1.0 / 256, EPS, ALU.mult, ALU.add))
                step(tt(t, ms, y, ALU.mult))
                step(stt(t, t, -0.5, y, ALU.mult, ALU.mult))
                step(stt(t, t, 1.5, y, ALU.add, ALU.mult))
                for n in range(n_ch):
                    stt(SV[:, n, :], SV[:, n, :], SM[:, 16 + n:17 + n], SGG[:, :], ALU.mult, ALU.mult
                        ).then_inc(S["sg_vn"], 1)
                for g in range(2):
                    dve.wait_ge(S["sg_mix"], base["sg_mix"] + g + 1)
                    o = TM[:, 2 + g, 0:w]
                    step(tt(o.rearrange("p (n q) -> p n q", q=P), pair(g, w).rearrange("p (n q) -> p n q", q=P),
                            SGB[:, g:g + 1, :].to_broadcast([P, n_ch, P]), ALU.add))
                    tt(o, o, SU[:, g, 0:w], ALU.mult).then_inc(S["sg_o"], 1)
                for g in range(2):
                    dve.wait_ge(S["sg_hi"], base["sg_hi"] + g + 1)
                    sub(F_lo[:, 4 + g, 0:w], TM[:, 2 + g, 0:w], F_hi[:, 4 + g, 0:w]).then_inc(S["sg_lo"], 1)
                base.advance(sg_step=c[0] - base["sg_step"], sg_y0=1, sg_vn=n_ch, sg_mix=2, sg_o=2, sg_hi=2, sg_lo=2)

            def merge(l, ph):
                begin(dve, ph, "pe", "act")
                w, b0 = width(l), done[0]
                n_mod_tiles, streams = mod_tiles(l)
                per = 2 * n_mod_tiles // KT

                def mod_tile(i, s):
                    dve.wait_ge(mod_loaded[s % 2], i * (8 * per) + (8 * ADA_T * l + 16 * (s // 2 + 1)))
                    for c in range(streams):
                        if first(i) and s == 0:
                            dve.wait_ge(S["cb_silu"], 2 * l + c + 3)
                        wait(dve, "mod_acc", i * (per * streams) + (2 * ADA_T * l + streams * s + c))
                        if s == 0:
                            wait(dve, "mod_fold", i * streams + KT * l)
                        k = per * c + s
                        nc.vector.tensor_tensor_reduce(MOD_P, MOD_W[s % 2], CB[c], 1.0, 0.0, ALU.mult, ALU.add,
                                                       MOD_ACC[:, k:k + 1]).then_inc(S["mod_acc"], 1)

                def fold(i):
                    dve.wait_ge(S["mod_acc"], i * (per * streams) + (2 * ADA_T * l + streams * per))
                    for c in range(streams):
                        tt(MOD[:, c, bass.ds(i * per + ADA_1, per)], MOD_ACC[:, per * c:per * (c + 1)],
                           ADAB[:, bass.ds(i * per + (ADA_T * l + ADA_1), per)], ALU.add).then_inc(S["mod_fold"], 1)

                def split_y(k):
                    dve.wait_ge(S["y_hi"], base["y_hi"] + k + 1)
                    sub(F_lo[:, k, 0:w], X3[:, k, 0:w], F_hi[:, k, 0:w]).then_inc(S["y_lo"], 1)

                def body(i, last):
                    for u in range(2):
                        b = b0 + (NBR + 1) * u
                        y = XY[:, bass.ds(i * (2 * T) + u * T, w)]
                        used(i, 10, b)
                        for s in range(NBR, per // 2):
                            mod_tile(i, u * (per // 2) + s - NBR)
                        for r in range(NBR):
                            b += 1
                            used(i, 10, b)
                            dve.wait_ge(S["gate_sig"], i * 8 + (base["gate_sig"] + NBR * u + r + 1))
                            dve.wait_ge(S["br_copy"], i * 8 + (base["br_copy"] + NBR * u + r + 1))
                            t = TM[:, 3 + r % 2, 0:w] if r else y
                            tt(t, SIG[:, r % 2, 0:w], BR[:, r, 0:w], ALU.mult).then_inc(S["gate_mul"], 1)
                            if r:
                                dve.wait_ge(S["gate_mul"], i * 8 + (base["gate_mul"] + NBR * u + r + 1))
                                if r > 1:
                                    dve.wait_ge(S["gate_add"], i * 6 + (base["gate_add"] + 3 * u + r - 1))
                                tt(y, y, t, ALU.add).then_inc(S["gate_add"], 1)
                            mod_tile(i, (u + 1) * (per // 2) - NBR + r)
                            if last and u == 1:
                                for k in range(2 * r, min(2 * r + 2, KT - 1)):
                                    split_y(k)
                    fold(i)

                repeat(dve, KT // 2, body, peel_last=True)
                done[0] += B_MERGE
                dve.wait_ge(S["mod_fold"], KT * l + KT // 2 * streams)
                split_y(KT - 1)
                one_plus_scale(SC2)
                base.advance(**MERGE_COUNTS)

            def out_tiles(w, gate, name, last_phase=False, squares=False, reloads=0):
                b0 = done[0]

                def body(i, final):
                    for u in range(2):
                        used(i, 2, b0 + u, stop=final)
                        if reloads and not first(i):
                            dve.wait_ge(S["x_reloaded"], 16 * reloads)
                        for c, (s0, sn) in enumerate(segs(w)):
                            x = XY[:, bass.ds(i * (2 * T) + (u * T + s0), sn)]
                            ins = stt(x, pair(u)[:, s0:s0 + sn], MOD[:, c, bass.ds(i * 2 + (gate + u), 1)], x,
                                      ALU.mult, ALU.add)
                        ins.then_inc(S[name], 1)
                        if squares:
                            if first(i) and u == 0:
                                continue
                            dve.wait_ge(S["sq"], i * 2 + (base["sq"] + u + 1))
                            if first(i):
                                tt(TT[:, 0:w], SQ[0][:, 0:w], SQ[1][:, 0:w], ALU.add).then_inc(S["sq_sum"], 1)
                            else:
                                dve.wait_ge(S["sq_sum"], i * 2 + (base["sq_sum"] + u - 1))
                                tt(TT[:, 0:w], TT[:, 0:w], SQ[u][:, 0:w], ALU.add).then_inc(S["sq_sum"], 1)

                repeat(dve, KT // 2, body, peel_last=last_phase)
                done[0] += KT
                base.advance(**{name: KT})
                if squares:
                    base.advance(sq_sum=KT - 1)

            def ffn(l, ph):
                w = width(l)
                taps = 2 * len(segs(w)) - 1
                for g, n in enumerate(GROUPS):
                    begin(dve, ph + 2 * g, "pe", "act")
                    b0, t0 = done[0], sum(GROUPS[:g])

                    def body(i, _):
                        for u in range(4):
                            used(i, 4, b0 + u)
                            s, gate = u // 2, u % 2
                            col = u // 2 + t0 + FFN_T * gate
                            o, ps = (UA, UG)[gate][:, s, :], pair(u)
                            dve.wait_ge(S["up_lin"], i * 4 + (base["up_lin"] + u + 1))
                            k = 0
                            for s0, sn in segs(w):
                                e = s0 + sn
                                for cw, oo, ii in ((C_W0, (s0 + 1, e), (s0, e - 1)), (C_W2, (s0, e - 1), (s0 + 1, e))):
                                    ins = stt(o[:, oo[0]:oo[1]], ps[:, ii[0]:ii[1]],
                                              PAR[:, bass.ds(i * 2 + (cw + col), 1)], o[:, oo[0]:oo[1]],
                                              ALU.mult, ALU.add)
                                    k += 1
                                    if k <= taps:
                                        ins.then_inc(S["up_tap"], 1)
                                        dve.wait_ge(S["up_tap"], i * (4 * taps) + (base["up_tap"] + taps * u + k))
                            ins.then_inc(S["up_conv"], 1)
                            if gate:
                                dve.wait_ge(S["up_conv"], i * 4 + (base["up_conv"] + u + 1))
                                dve.wait_ge(S["up_act"], i * 2 + (base["up_act"] + s + 1))
                                tt(UA[:, s, 0:w], UA[:, s, 0:w], UG[:, s, 0:w], ALU.mult).then_inc(S["up_mul"], 1)
                                dve.wait_ge(S["up_mul"], i * 2 + (base["up_mul"] + s + 1))
                                dve.wait_ge(S["up_hi"], i * 2 + (base["up_hi"] + s + 1))
                                fl, fh = (f[:, bass.ds(i * 2 + s, 1), 0:w].rearrange("p a t -> p (a t)")
                                          for f in (F_lo, F_hi))
                                sub(fl, UA[:, s, 0:w], fh).then_inc(S["up_lo"], 1)

                    repeat(dve, n // 2, body)
                    done[0] += 2 * n
                    base.advance(**up_counts(w, n))
                    end(dve, "dve")
                    begin(dve, ph + 2 * g + 1, "pe", "act")
                    out_tiles(w, G2, "down_add", l == DEPTH - 1 and g == len(GROUPS) - 1,
                              l < DEPTH - 1 and g == len(GROUPS) - 1)
                    end(dve, "dve")

            nc.vector.memset(EPSB, EPS)
            for l in range(DEPTH):
                p0, w = PHASES * l, width(l)
                if l == 0:
                    ada()
                one_plus_scale(SC1 + ADA_T * l)
                end(dve, "dve")
                if l == 0:
                    for b in range(2):
                        dve.wait_ge(w_loaded[b], 16)
                        split_lo(b, b + 1)
                norm(p0 + PH_NORM1, T, own_squares=l == 0)
                halve_gains(l)
                end(dve, "dve")
                for kind, ph in (("mla", PH_MLA), ("na", PH_NA), ("gs", PH_GS)):
                    in_phase(kind, l, p0 + ph)
                    end(dve, "dve")
                    attention(kind, l, p0 + ph + 1)
                    end(dve, "dve")
                gating(l, p0 + PH_SG)
                end(dve, "dve")
                merge(l, p0 + PH_MERGE)
                end(dve, "dve")
                begin(dve, p0 + PH_OUT, "pe", "act")
                dve.wait_ge(S["x_head"], 16 * (l + 1))
                out_tiles(w, G1, "out_add", squares=True, reloads=l + 1)
                end(dve, "dve")
                norm(p0 + PH_NORM2, w)
                end(dve, "dve")
                ffn(l, p0 + PH_FFN)


def kernel(**inputs):
    import numpy as np
    import concourse.bacc as bacc
    from concourse.bass_utils import run_bass_kernel_spmd

    a = {k: np.asarray(v) for k, v in inputs.items()}
    f = np.float32

    def feat(v):
        return v.reshape(-1, P, v.shape[-1]).transpose(1, 0, 2)

    def pad_rows(v, n):
        return np.concatenate([v, np.zeros((n - v.shape[0],) + v.shape[1:], f)], 0)

    def col_tile(w):
        return feat(w).reshape(P, -1)

    def fill(w):
        return np.concatenate([w, np.zeros((P, BW - w.shape[1]), f)], 1)

    x_in = np.concatenate([feat(a["x"][0].T), feat(a["ctx"][0].T)], 2).reshape(P, KT * T)
    cc_in = np.stack([feat(a["c"].T)[..., 0], feat(a["c_ctx"][:, None])[..., 0]], 2)
    w_ada = np.stack([col_tile(a["w_ada"][0][:, P * j:P * j + P]) for j in range(KT)])
    w_mod = np.concatenate([a["w_ada"][l].T.reshape(ADA_T, P, D) for l in range(DEPTH)])
    cb_in = np.stack([np.tile(a["c"], (P, 1)), np.tile(a["c_ctx"], (P, 1))])
    adab_in = np.concatenate([a["b_ada"][l].reshape(-1, P).T for l in range(DEPTH)], 1)
    blocks, pars, sgg, sgw, sgb, bias = [], [], [], [], [], []
    o_mla, o_sg, o_gqa = 768, 768 + 480, 768 + 480 + 512
    qc, qr = np.arange(P) // 8, np.arange(P) % 8
    kc, kr = np.arange(384) // 8, np.arange(384) % 8
    dr = kr[None, :] - qr[:, None] + 7

    def window(query0, key0, n):
        q, k = query0 + qc[:, None], key0 + kc[None, :n]
        start = np.clip(q - 8, 0, GRID_W - 16)
        ok = (k >= start) & (k < start + 16)
        return np.clip(k - q + 15, 0, 30), np.where(ok, 0.0, -1e30).astype(f)

    wins = [window(0, 0, 256), window(16, 0, 384), window(48, 32, 256)]
    mask_na = np.concatenate([m for _, m in wins], 1)
    for l in range(DEPTH):
        wi = a["w_in"][l]
        cols = lambda c, n=P: wi[:, c:c + n]
        gq = wi[:, o_gqa:o_gqa + 256].reshape(D, 2, 2, HD)
        ckv1 = np.concatenate([cols(o_mla + 384, 64), cols(o_mla + 448, 32), np.zeros((D, 32), f)], 1)
        b = [col_tile(cols(o_mla + 256)), col_tile(ckv1), col_tile(cols(o_mla)), col_tile(cols(o_mla + P))]
        uq = a["mla_w_uq"][l].reshape(256, NHEAD, MLA_K)
        uq = np.concatenate([uq, np.zeros((256, NHEAD, P - MLA_K), f)], 2)
        b.append(np.concatenate([col_tile(uq[:, h]) for h in range(NHEAD)], 1))
        ukv = pad_rows(a["mla_w_ukv"][l], 256).reshape(256, NHEAD, 2, HD)
        b.append(np.concatenate([feat(ukv[:, :, e].reshape(256, 256)).reshape(P, 512) for e in range(2)], 1))
        b += [col_tile(cols(P * t)) for t in range(4)]
        b += list(feat(wi[:, 512:768]).reshape(P, 2, BW).transpose(1, 0, 2))
        b += [col_tile(gq[:, :, r].reshape(D, P)) for r in range(2)] + [col_tile(cols(o_gqa + 256))]
        vs = np.concatenate([wi[:, o_gqa + 384:o_gqa + 512], wi[:, o_sg + 256:o_sg + 512]], 1)
        b += [fill(v) for v in feat(vs).reshape(P, 4, 768).transpose(1, 0, 2)]
        b += [col_tile(cols(o_sg + P * t)) for t in range(2)]
        for m in range(KT):
            c = slice(P * m, P * m + P)
            b.append(np.concatenate([col_tile(a["w_branch"][l, i][:, c]) for i in range(NBR)], 1))
            b += [col_tile(a["w_gate"][l, i][:, c]) for i in range(NBR)]
        b += [col_tile(a["w_out"][l][:, P * m:P * m + P]) for m in range(KT)]
        t0 = 0
        for n in GROUPS:
            for t in range(t0, t0 + n):
                for e in range(2):
                    c = P * (t + FFN_T * e)
                    b.append(col_tile(a["w_up"][l][:, c:c + P]))
            b += [fill(col_tile(a["w_down"][l][P * t0:P * (t0 + n), P * m:P * m + P])) for m in range(KT)]
            t0 += n
        blocks += b
        ft = lambda v: v.reshape(-1, P).T
        pr = np.zeros((P, N_PAR), f)
        for c, name in ((C_NAQ, "na_q_norm"), (C_NAK, "na_k_norm"), (C_GQ, "gqa_q_norm"), (C_GK, "gqa_k_norm")):
            pr[:, c] = np.tile(a[name][l], 2)
        pr[:MLA_K, C_MQ], pr[:MLA_K, C_MK] = a["mla_q_norm"][l], a["mla_k_norm"][l]
        pr[:, C_MK2] = np.tile(a["mla_k_norm"][l][:HD], 2)
        pr[:, C_CQ:C_CQ + 2] = ft(a["mla_cq_norm"][l])
        pr[:, C_CKV:C_CKV + 2] = ft(pad_rows(a["mla_ckv_norm"][l], 256))
        pr[:, C_BG:C_BG + NBR * KT] = ft(a["b_gate"][l].reshape(-1))
        for i, c in enumerate((C_W0, C_W1, C_W2)):
            pr[:, c:c + 2 * FFN_T] = ft(a["conv_w"][l, i])
        pr[:, C_CB:C_CB + 2 * FFN_T] = ft(a["conv_b"][l])
        pars.append(pr)
        sgg.append(np.tile(a["sg_v_norm"][l], (P, 1)))
        sgw.append(a["sg_w_s"][l].transpose(2, 0, 1))
        sgb.append(np.repeat(a["sg_b_s"][l].reshape(2, 2, 1, P), HD, 2).reshape(2, P, P).transpose(1, 0, 2))
        rpb = a["na_rpb"][l]
        bias.append(np.concatenate([rpb[:, dr[:, :d.shape[1]], d] for d, _ in wins], 2).transpose(1, 0, 2))

    idx = np.arange(P)
    mats = np.zeros((6, P, P), f)
    mats[M_ONE], mats[M_256], mats[M_192] = 1 / D, 1 / 256, f(1 / 192)
    mats[M_64] = (idx[:, None] // HD == idx[None, :] // HD) / HD
    mats[M_MLA, :64, :64], mats[M_MLA, 64:96, 64:96] = 1 / 64, 1 / 32
    mats[M_ID] = np.eye(P)
    t = np.arange(SEQ)
    rope = np.zeros((P, 4, SEQ), f)
    for e, (first, dim, rows) in enumerate(((0, HD, P), (64, 32, 96))):
        half = dim // 4
        inv = f(10000.0) ** (-np.arange(half, dtype=f) / f(half))
        for p in range(first, rows):
            d = (p - first) % dim
            pos = (t // GRID_W if d < dim // 2 else t % GRID_W).astype(f)
            ang = pos * inv[d % half]
            sign = -1 if d % (dim // 2) < half else 1
            rope[p, 2 * e], rope[p, 2 * e + 1] = np.cos(ang), sign * np.sin(ang)

    arrays = dict(x_in=x_in, cc_in=cc_in, cb_in=cb_in, w_ada=w_ada, w_mod=w_mod, w_all=np.stack(blocks), par=np.stack(pars),
                  sg_gain=np.stack(sgg), sg_ws=np.stack(sgw), sg_bs=np.stack(sgb), bias_na=np.stack(bias),
                  mask_na=mask_na, adab_in=adab_in, mats_in=mats.transpose(1, 0, 2), rope_in=rope)
    nc = bacc.Bacc("TRN2", target_bir_lowering=False, num_devices=1)
    args = {}
    for name in arrays:
        arrays[name] = np.ascontiguousarray(arrays[name], dtype=f)
        args[name] = nc.dram_tensor(name, arrays[name].shape, F32, kind="ExternalInput").ap()
    out = nc.dram_tensor("out", (P, KT, SEQ), F32, kind="ExternalOutput").ap()
    hybrid_backbone_kernel(nc, out=out, **args)
    r = run_bass_kernel_spmd(nc, [arrays], core_ids=[0])
    return r.results[0]["out"].transpose(2, 1, 0).reshape(1, SEQ, D)
```
